# Optimizing a Trainium2 kernel written in Bass

```python
import math
import jax
import jax.numpy as jnp
from jax import lax
import numpy as np

D_MODEL = 1024
BATCH = 1
SEQ = 1024
DEPTH = 4

GRID_W = 64
CTX_LEN = 256
N_MIXERS = 4
N_GDN = (DEPTH + 3) // 4
N_RWKV = (DEPTH + 2) // 4
N_GLA = (DEPTH + 1) // 4
N_MLA = DEPTH // 4
DEEPNORM_ALPHA = (2.0 * DEPTH) ** 0.25
DEEPNORM_BETA = (8.0 * DEPTH) ** -0.25
CHUNK = 64
LN_EPS = 1e-5
RMS_EPS = 1e-6

GDN_HEADS = 8
GDN_DK = 128
GDN_DV = 128
GDN_CONV = 5
GDN_QK = GDN_HEADS * GDN_DK
GDN_V = GDN_HEADS * GDN_DV
GDN_IN = 2 * GDN_QK + 2 * GDN_V + 4 * GDN_HEADS

RWKV_HEAD = 64
RWKV_HEADS = D_MODEL // RWKV_HEAD
RWKV_DECAY_RANK = 64
RWKV_ICL_RANK = 64
RWKV_GN_EPS = 64e-5

GLA_HEADS = 4
GLA_DK = D_MODEL // 2 // GLA_HEADS
GLA_DV = D_MODEL // GLA_HEADS
GLA_GATE_RANK = 16
GLA_GATE_TAU = 16.0
GLA_QK = GLA_HEADS * GLA_DK
GLA_V = GLA_HEADS * GLA_DV
GLA_IN = 2 * GLA_QK + 2 * GLA_V + 2 * GLA_GATE_RANK

MLA_HEADS = 8
MLA_Q_LORA = 384
MLA_KV_LORA = 256
MLA_NOPE = 128
MLA_ROPE = 64
MLA_DV = 128
MLA_IN = MLA_Q_LORA + MLA_KV_LORA + MLA_ROPE + MLA_HEADS * MLA_DV
MLA_SCALE = (MLA_NOPE + MLA_ROPE) ** -0.5
Q_BLOCK = 128
ROPE_BASE = 10000.0

kernel_name = 'hybrid_bidir_gdn_rwkv7_gla_mla_dit'

F32 = jnp.float32

def layer_norm(x, g, b):
    xf = x.astype(F32)
    xc = xf - jnp.mean(xf, -1, keepdims=True)
    y = xc * lax.rsqrt(jnp.mean(xc * xc, -1, keepdims=True) + LN_EPS)
    return (y * g.astype(F32) + b.astype(F32)).astype(x.dtype)

def rms_norm(x, g):
    xf = x.astype(F32)
    y = xf * lax.rsqrt(jnp.mean(xf * xf, -1, keepdims=True) + RMS_EPS)
    return (y * g.astype(F32)).astype(x.dtype)

def l2_normalize(x):
    xf = x.astype(F32)
    return xf * lax.rsqrt(jnp.sum(xf * xf, -1, keepdims=True) + RMS_EPS)

def to_heads(t, n_heads):
    t = t.reshape(*t.shape[:-1], n_heads, -1)
    return jnp.swapaxes(t, -3, -2)

def from_heads(t):
    t = jnp.swapaxes(t, -3, -2)
    return t.reshape(*t.shape[:-2], -1)

def flip_seq(t):
    return jnp.flip(t, -2)

def centred_depthwise_conv(u, w):
    k = w.shape[0]
    return lax.conv_general_dilated(u, w[:, None, :].astype(u.dtype), window_strides=(1,),
                                    padding=[(k // 2, k // 2)],
                                    dimension_numbers=('NWC', 'WIO', 'NWC'),
                                    feature_group_count=u.shape[-1])

def centred_token_shift(u):
    prev = jnp.pad(u[:, :-1], ((0, 0), (1, 0), (0, 0)))
    nxt = jnp.pad(u[:, 1:], ((0, 0), (0, 1), (0, 0)))
    return 0.5 * (prev + nxt) - u

def axial_rope_tables(n_tokens):
    rows = n_tokens // GRID_W
    row = jnp.repeat(jnp.arange(rows, dtype=F32), GRID_W)
    col = jnp.tile(jnp.arange(GRID_W, dtype=F32), rows)
    n_freq = MLA_ROPE // 4
    inv_freq = ROPE_BASE ** (-jnp.arange(n_freq, dtype=F32) / n_freq)
    ang = jnp.concatenate([row[:, None] * inv_freq, col[:, None] * inv_freq], axis=-1)
    return jnp.cos(ang), jnp.sin(ang)

def apply_rope(t, cos, sin):
    t1, t2 = jnp.split(t, 2, axis=-1)
    cos = cos.astype(t.dtype)
    sin = sin.astype(t.dtype)
    return jnp.concatenate([t1 * cos - t2 * sin, t1 * sin + t2 * cos], axis=-1)

def gated_delta_rule(q, k, v, beta, g, state):
    b, h, l, dk = q.shape
    dv = v.shape[-1]
    n = l // CHUNK
    q, k, v = (t.reshape(b, h, n, CHUNK, -1) for t in (q, k, v))
    beta, g = (t.reshape(b, h, n, CHUNK) for t in (beta, g))
    gc = jnp.cumsum(g, axis=-1)
    causal = jnp.tril(jnp.ones((CHUNK, CHUNK), bool))
    strict = jnp.tril(jnp.ones((CHUNK, CHUNK), bool), -1)
    decay = jnp.exp(jnp.where(causal, gc[..., :, None] - gc[..., None, :], -jnp.inf))
    kb = k * beta[..., None]
    lower = jnp.where(strict, jnp.einsum('bhnid,bhnjd->bhnij', kb, k) * decay, 0.0)
    rhs = jnp.concatenate([v * beta[..., None], kb * jnp.exp(gc)[..., None]], axis=-1)
    sol = lax.linalg.triangular_solve(lower, rhs, left_side=True, lower=True, unit_diagonal=True)
    u0, wk = sol[..., :dv], sol[..., dv:]
    qk = jnp.einsum('bhnid,bhnjd->bhnij', q, k) * decay
    qg = q * jnp.exp(gc)[..., None]
    kd = k * jnp.exp(gc[..., -1:] - gc)[..., None]
    gl = jnp.exp(gc[..., -1])

    def step(s, inp):
        u0_c, wk_c, qk_c, qg_c, kd_c, gl_c = inp
        u = u0_c - jnp.einsum('bhck,bhkv->bhcv', wk_c, s)
        o = jnp.einsum('bhck,bhkv->bhcv', qg_c, s) + jnp.einsum('bhij,bhjv->bhiv', qk_c, u)
        s = s * gl_c[..., None, None] + jnp.einsum('bhck,bhcv->bhkv', kd_c, u)
        return s, o

    xs = tuple(jnp.moveaxis(t, 2, 0) for t in (u0, wk, qk, qg, kd, gl))
    state, o = lax.scan(step, state, xs)
    return jnp.moveaxis(o, 0, 2).reshape(b, h, l, dv), state

def gdn_mixer(h, hc, w_in, conv_w, a_log, dt_bias, norm_g, w_out, need_ctx):
    def project(u):
        p = u @ w_in
        qkv = jax.nn.silu(centred_depthwise_conv(p[..., :2 * GDN_QK + GDN_V], conv_w))
        q = l2_normalize(to_heads(qkv[..., :GDN_QK], GDN_HEADS)) * GDN_DK ** -0.5
        k = l2_normalize(to_heads(qkv[..., GDN_QK:2 * GDN_QK], GDN_HEADS))
        v = to_heads(qkv[..., 2 * GDN_QK:], GDN_HEADS).astype(F32)
        z = p[..., 2 * GDN_QK + GDN_V:2 * GDN_QK + 2 * GDN_V]
        ab = p[..., 2 * GDN_QK + 2 * GDN_V:].astype(F32)
        ab = ab.reshape(*ab.shape[:-1], 2, 2, GDN_HEADS)
        ab = jnp.swapaxes(jnp.moveaxis(ab, (2, 3), (0, 1)), -1, -2)
        beta = jax.nn.sigmoid(ab[:, 0])
        g = -jnp.exp(a_log.astype(F32))[:, None, :, None] * jax.nn.softplus(
            ab[:, 1] + dt_bias.astype(F32)[:, None, :, None])
        return q, k, v, z, beta, g

    def bidir(q, k, v, beta, g, s_f, s_b):
        o_f, s_f = gated_delta_rule(q, k, v, beta[0], g[0], s_f)
        o_b, s_b = gated_delta_rule(flip_seq(q), flip_seq(k), flip_seq(v),
                                    jnp.flip(beta[1], -1), jnp.flip(g[1], -1), s_b)
        return o_f + flip_seq(o_b), s_f, s_b

    def finish(o, z):
        o = rms_norm(jnp.swapaxes(o, 1, 2), norm_g)
        gate = jax.nn.silu(z.astype(F32)).reshape(o.shape)
        return (o * gate).reshape(*o.shape[:2], -1).astype(h.dtype) @ w_out

    zero = jnp.zeros((h.shape[0], GDN_HEADS, GDN_DK, GDN_DV), F32)
    qc, kc, vc, zc, bc, gcx = project(hc)
    oc, s_f, s_b = bidir(qc, kc, vc, bc, gcx, zero, zero)
    q, k, v, z, bt, g = project(h)
    o, _, _ = bidir(q, k, v, bt, g, s_f, s_b)
    y = finish(o, z)
    yc = finish(oc, zc) if need_ctx else None
    return y, yc

def rwkv7_scan(r, w, k, v, kk, kka, state):
    def step(s, inp):
        r_t, w_t, k_t, v_t, kk_t, kka_t = inp
        sa = jnp.einsum('bhvk,bhk->bhv', s, kk_t)
        s = s * w_t[:, :, None, :] - sa[..., None] * kka_t[:, :, None, :] + v_t[..., None] * k_t[:, :, None, :]
        return s, jnp.einsum('bhvk,bhk->bhv', s, r_t)

    xs = tuple(jnp.moveaxis(t, 2, 0) for t in (r, w, k, v, kk, kka))
    state, y = lax.scan(step, state, xs)
    return jnp.moveaxis(y, 0, 2), state

def rwkv7_mixer(h, hc, mu, w_rkvz, w0, w1, w2, a0, a1, a2, k_k, k_a, r_k, gn_g, gn_b, w_out, need_ctx):
    def project(u):
        xx = centred_token_shift(u)
        xr, xw, xk, xv, xa, xg = (u + xx * mu[i] for i in range(6))
        r = to_heads(xr @ w_rkvz[0], RWKV_HEADS).astype(F32)
        k = xk @ w_rkvz[1]
        v = to_heads(xv @ w_rkvz[2], RWKV_HEADS).astype(F32)
        z = xg @ w_rkvz[3]
        lw = jnp.tanh(jnp.einsum('bld,ndr->nblr', xw, w1))
        wlog = (w0[:, None, None, :] + jnp.einsum('nblr,nrd->nbld', lw, w2)).astype(F32)
        decay = jnp.exp(-jnp.exp(-jax.nn.softplus(-wlog) - 0.5))
        a = jax.nn.sigmoid((a0[:, None, None, :] + jnp.einsum(
            'nblr,nrd->nbld', jnp.einsum('bld,ndr->nblr', xa, a1), a2)).astype(F32))
        kk = l2_normalize(to_heads(k * k_k, RWKV_HEADS))
        k_dir = to_heads(k.astype(F32)[None] * (1.0 + (a - 1.0) * k_a.astype(F32)), RWKV_HEADS)
        kka = kk[None] * to_heads(a, RWKV_HEADS)
        return r, to_heads(decay, RWKV_HEADS), k_dir, v, kk, kka, z

    def bidir(r, w, kd, v, kk, kka, s_f, s_b):
        y_f, s_f = rwkv7_scan(r, w[0], kd[0], v, kk, kka[0], s_f)
        y_b, s_b = rwkv7_scan(*(flip_seq(t) for t in (r, w[1], kd[1], v, kk, kka[1])), s_b)
        return y_f + flip_seq(y_b), s_f, s_b

    def finish(y, r, kd, v, z):
        mean = jnp.mean(y, -1, keepdims=True)
        yc_ = y - mean
        var = jnp.mean(yc_ * yc_, -1, keepdims=True)
        g_ = gn_g.astype(F32).reshape(RWKV_HEADS, 1, RWKV_HEAD)
        b_ = gn_b.astype(F32).reshape(RWKV_HEADS, 1, RWKV_HEAD)
        yn = yc_ * lax.rsqrt(var + RWKV_GN_EPS) * g_ + b_
        bonus = jnp.sum(jnp.sum(r[None] * kd * r_k.astype(F32)[:, None, :], -1, keepdims=True), 0) * v
        out = from_heads(yn + bonus) * jax.nn.silu(z.astype(F32))
        return out.astype(h.dtype) @ w_out

    zero = jnp.zeros((h.shape[0], RWKV_HEADS, RWKV_HEAD, RWKV_HEAD), F32)
    rc, wc, kdc, vc, kkc, kkac, zc = project(hc)
    yc, s_f, s_b = bidir(rc, wc, kdc, vc, kkc, kkac, zero, zero)
    r, w, kd, v, kk, kka, z = project(h)
    y, _, _ = bidir(r, w, kd, v, kk, kka, s_f, s_b)
    out = finish(y, r, kd, v, z)
    out_c = finish(yc, rc, kdc, vc, zc) if need_ctx else None
    return out, out_c

def gla_chunked(q, k, v, g, state):
    b, h, l, dk = q.shape
    dv = v.shape[-1]
    n = l // CHUNK
    q, k, v, g = (t.reshape(b, h, n, CHUNK, -1) for t in (q, k, v, g))
    bc = jnp.cumsum(g, axis=-2)
    ref = bc[..., CHUNK // 2:CHUNK // 2 + 1, :]
    causal = jnp.tril(jnp.ones((CHUNK, CHUNK), bool))
    att = jnp.einsum('bhnid,bhnjd->bhnij', q * jnp.exp(bc - ref), k * jnp.exp(ref - bc))
    att = jnp.where(causal, att, 0.0)
    o_intra = jnp.einsum('bhnij,bhnjv->bhniv', att, v)
    qg = q * jnp.exp(bc)
    kd = k * jnp.exp(bc[..., -1:, :] - bc)
    gl = jnp.exp(bc[..., -1, :])

    def step(s, inp):
        qg_c, kd_c, v_c, gl_c = inp
        o = jnp.einsum('bhck,bhkv->bhcv', qg_c, s)
        s = s * gl_c[..., None] + jnp.einsum('bhck,bhcv->bhkv', kd_c, v_c)
        return s, o

    xs = tuple(jnp.moveaxis(t, 2, 0) for t in (qg, kd, v, gl))
    state, o_inter = lax.scan(step, state, xs)
    o = o_intra + jnp.moveaxis(o_inter, 0, 2)
    return o.reshape(b, h, l, dv), state

def gla_mixer(h, hc, w_in, w_g2, b_g, norm_g, w_out, need_ctx):
    def project(u):
        p = u @ w_in
        q = to_heads(p[..., :GLA_QK], GLA_HEADS).astype(F32) * GLA_DK ** -0.5
        k = to_heads(p[..., GLA_QK:2 * GLA_QK], GLA_HEADS).astype(F32)
        v = to_heads(p[..., 2 * GLA_QK:2 * GLA_QK + GLA_V], GLA_HEADS).astype(F32)
        z = p[..., 2 * GLA_QK + GLA_V:2 * GLA_QK + 2 * GLA_V]
        gr = p[..., 2 * GLA_QK + 2 * GLA_V:]
        gr = gr.reshape(*gr.shape[:-1], 2, GLA_GATE_RANK)
        glog = jax.nn.log_sigmoid((jnp.einsum('blnr,nrk->nblk', gr, w_g2)
                                   + b_g[:, None, None, :]).astype(F32)) / GLA_GATE_TAU
        return q, k, v, z, to_heads(glog, GLA_HEADS)

    def bidir(q, k, v, g, s_f, s_b):
        o_f, s_f = gla_chunked(q, k, v, g[0], s_f)
        o_b, s_b = gla_chunked(flip_seq(q), flip_seq(k), flip_seq(v), flip_seq(g[1]), s_b)
        return o_f + flip_seq(o_b), s_f, s_b

    def finish(o, z):
        o = rms_norm(jnp.swapaxes(o, 1, 2), norm_g)
        gate = jax.nn.silu(z.astype(F32)).reshape(o.shape)
        return (o * gate).reshape(*o.shape[:2], -1).astype(h.dtype) @ w_out

    zero = jnp.zeros((h.shape[0], GLA_HEADS, GLA_DK, GLA_DV), F32)
    qc, kc, vc, zc, gcx = project(hc)
    oc, s_f, s_b = bidir(qc, kc, vc, gcx, zero, zero)
    q, k, v, z, g = project(h)
    o, _, _ = bidir(q, k, v, g, s_f, s_b)
    y = finish(o, z)
    yc = finish(oc, zc) if need_ctx else None
    return y, yc

def mla_attend(qn, qr, kn, kr, v):
    s = (jnp.einsum('bqhd,bkhd->bhqk', qn, kn) + jnp.einsum('bqhd,bkd->bhqk', qr, kr)).astype(F32) * MLA_SCALE
    p = jax.nn.softmax(s, axis=-1)
    return jnp.einsum('bhqk,bkhd->bqhd', p.astype(v.dtype), v)

def mla_mixer(h, hc, w_in, q_norm, kv_norm, w_uq, w_ukv, w_out, cos, sin, need_ctx):
    def project(u, rotate):
        b, l, _ = u.shape
        p = u @ w_in
        o1 = MLA_Q_LORA
        o2 = o1 + MLA_KV_LORA
        o3 = o2 + MLA_ROPE
        q = (rms_norm(p[..., :o1], q_norm) @ w_uq).reshape(b, l, MLA_HEADS, MLA_NOPE + MLA_ROPE)
        kv = (rms_norm(p[..., o1:o2], kv_norm) @ w_ukv).reshape(b, l, MLA_HEADS, MLA_NOPE + MLA_DV)
        q_nope, q_rope = q[..., :MLA_NOPE], q[..., MLA_NOPE:]
        k_nope, v = kv[..., :MLA_NOPE], kv[..., MLA_NOPE:]
        k_rope = p[..., o2:o3]
        if rotate:
            q_rope = apply_rope(q_rope, cos[:, None, :], sin[:, None, :])
            k_rope = apply_rope(k_rope, cos, sin)
        return q_nope, q_rope, k_nope, k_rope, v, p[..., o3:]

    def finish(o, z):
        return (o * jax.nn.silu(z)) @ w_out

    b, l, _ = h.shape
    qn_c, qr_c, kn_c, kr_c, v_c, z_c = project(hc, False)
    qn, qr, kn, kr, v, z = project(h, True)
    kn_all = jnp.concatenate([kn, kn_c], axis=1)
    kr_all = jnp.concatenate([kr, kr_c], axis=1)
    v_all = jnp.concatenate([v, v_c], axis=1)
    nb = l // Q_BLOCK

    def blocks(t):
        return jnp.moveaxis(t.reshape(b, nb, Q_BLOCK, *t.shape[2:]), 1, 0)

    o = lax.map(lambda qb: mla_attend(qb[0], qb[1], kn_all, kr_all, v_all), (blocks(qn), blocks(qr)))
    o = jnp.moveaxis(o, 0, 1).reshape(b, l, MLA_HEADS * MLA_DV)
    y = finish(o, z)
    if need_ctx:
        oc = mla_attend(qn_c, qr_c, kn_c, kr_c, v_c).reshape(b, -1, MLA_HEADS * MLA_DV)
        return y, finish(oc, z_c)
    return y, None

def setup_inputs(seed: int = 0) -> dict:
    key = jax.random.key(seed)
    ks = list(jax.random.split(key, 48))
    d = D_MODEL

    def nrm(shape, scale):
        return scale * jax.random.normal(ks.pop(), shape, F32)

    def unif(shape, lo, hi):
        return jax.random.uniform(ks.pop(), shape, F32, lo, hi)

    def out_scale(fan_in):
        return DEEPNORM_BETA * fan_in ** -0.5

    dt = jnp.exp(unif((N_GDN, 2, GDN_HEADS), math.log(1e-3), math.log(1e-1)))
    return {
        'x': nrm((BATCH, SEQ, d), 1.0),
        'c': nrm((BATCH, d), 1.0),
        'ctx': nrm((BATCH, CTX_LEN, d), 1.0),
        'c_ctx': nrm((d,), 1.0),
        'ada_w': nrm((DEPTH, d, 3 * d), 0.5 * d ** -0.5),
        'ada_b': nrm((DEPTH, 3 * d), 0.02),
        'ln_g': 1.0 + nrm((DEPTH, d), 0.02),
        'ln_b': nrm((DEPTH, d), 0.02),
        'gdn_w_in': nrm((N_GDN, d, GDN_IN), d ** -0.5),
        'gdn_conv': nrm((N_GDN, GDN_CONV, 2 * GDN_QK + GDN_V), GDN_CONV ** -0.5),
        'gdn_a_log': jnp.log(unif((N_GDN, 2, GDN_HEADS), 1.0, 16.0)),
        'gdn_dt_bias': dt + jnp.log(-jnp.expm1(-dt)),
        'gdn_norm': 1.0 + nrm((N_GDN, GDN_DV), 0.02),
        'gdn_w_out': nrm((N_GDN, GDN_V, d), out_scale(GDN_V)),
        'rwkv_mu': unif((N_RWKV, 6, d), 0.0, 1.0),
        'rwkv_w_rkvz': nrm((N_RWKV, 4, d, d), d ** -0.5),
        'rwkv_w0': unif((N_RWKV, 2, d), -6.0, 0.0),
        'rwkv_w1': nrm((N_RWKV, 2, d, RWKV_DECAY_RANK), d ** -0.5),
        'rwkv_w2': nrm((N_RWKV, 2, RWKV_DECAY_RANK, d), 0.1 * RWKV_DECAY_RANK ** -0.5),
        'rwkv_a0': nrm((N_RWKV, 2, d), 0.1),
        'rwkv_a1': nrm((N_RWKV, 2, d, RWKV_ICL_RANK), d ** -0.5),
        'rwkv_a2': nrm((N_RWKV, 2, RWKV_ICL_RANK, d), 0.1 * RWKV_ICL_RANK ** -0.5),
        'rwkv_k_k': 0.85 + nrm((N_RWKV, d), 0.02),
        'rwkv_k_a': 1.0 + nrm((N_RWKV, d), 0.02),
        'rwkv_r_k': nrm((N_RWKV, RWKV_HEADS, RWKV_HEAD), 0.1),
        'rwkv_gn_g': 1.0 + nrm((N_RWKV, d), 0.02),
        'rwkv_gn_b': nrm((N_RWKV, d), 0.02),
        'rwkv_w_out': nrm((N_RWKV, d, d), out_scale(d)),
        'gla_w_in': nrm((N_GLA, d, GLA_IN), d ** -0.5),
        'gla_w_g2': nrm((N_GLA, 2, GLA_GATE_RANK, GLA_QK), GLA_GATE_RANK ** -0.5),
        'gla_b_g': unif((N_GLA, 2, GLA_QK), 0.0, 4.0),
        'gla_norm': 1.0 + nrm((N_GLA, GLA_DV), 0.02),
        'gla_w_out': nrm((N_GLA, GLA_V, d), out_scale(GLA_V)),
        'mla_w_in': nrm((N_MLA, d, MLA_IN), d ** -0.5),
        'mla_q_norm': 1.0 + nrm((N_MLA, MLA_Q_LORA), 0.02),
        'mla_kv_norm': 1.0 + nrm((N_MLA, MLA_KV_LORA), 0.02),
        'mla_w_uq': nrm((N_MLA, MLA_Q_LORA, MLA_HEADS * (MLA_NOPE + MLA_ROPE)), MLA_Q_LORA ** -0.5),
        'mla_w_ukv': nrm((N_MLA, MLA_KV_LORA, MLA_HEADS * (MLA_NOPE + MLA_DV)), MLA_KV_LORA ** -0.5),
        'mla_w_out': nrm((N_MLA, MLA_HEADS * MLA_DV, d), out_scale(MLA_HEADS * MLA_DV)),
    }

def reference(x, c, ctx, c_ctx, ada_w, ada_b, ln_g, ln_b,
              gdn_w_in, gdn_conv, gdn_a_log, gdn_dt_bias, gdn_norm, gdn_w_out,
              rwkv_mu, rwkv_w_rkvz, rwkv_w0, rwkv_w1, rwkv_w2, rwkv_a0, rwkv_a1, rwkv_a2,
              rwkv_k_k, rwkv_k_a, rwkv_r_k, rwkv_gn_g, rwkv_gn_b, rwkv_w_out,
              gla_w_in, gla_w_g2, gla_b_g, gla_norm, gla_w_out,
              mla_w_in, mla_q_norm, mla_kv_norm, mla_w_uq, mla_w_ukv, mla_w_out):
    cos, sin = axial_rope_tables(x.shape[1])
    xc = ctx
    silu_c = jax.nn.silu(c)
    silu_cc = jax.nn.silu(c_ctx)
    for i in range(DEPTH):
        kind, j = i % N_MIXERS, i // N_MIXERS
        need_ctx = i < DEPTH - 1
        shift, scale, gate = jnp.split(silu_c @ ada_w[i] + ada_b[i], 3, axis=-1)
        shift_c, scale_c, gate_c = jnp.split(silu_cc @ ada_w[i] + ada_b[i], 3, axis=-1)
        h = x * (1.0 + scale[:, None, :]) + shift[:, None, :]
        hc = xc * (1.0 + scale_c) + shift_c
        if kind == 0:
            y, yc = gdn_mixer(h, hc, gdn_w_in[j], gdn_conv[j], gdn_a_log[j], gdn_dt_bias[j],
                              gdn_norm[j], gdn_w_out[j], need_ctx)
        elif kind == 1:
            y, yc = rwkv7_mixer(h, hc, rwkv_mu[j], rwkv_w_rkvz[j], rwkv_w0[j], rwkv_w1[j], rwkv_w2[j],
                                rwkv_a0[j], rwkv_a1[j], rwkv_a2[j], rwkv_k_k[j], rwkv_k_a[j],
                                rwkv_r_k[j], rwkv_gn_g[j], rwkv_gn_b[j], rwkv_w_out[j], need_ctx)
        elif kind == 2:
            y, yc = gla_mixer(h, hc, gla_w_in[j], gla_w_g2[j], gla_b_g[j], gla_norm[j],
                              gla_w_out[j], need_ctx)
        else:
            y, yc = mla_mixer(h, hc, mla_w_in[j], mla_q_norm[j], mla_kv_norm[j], mla_w_uq[j],
                              mla_w_ukv[j], mla_w_out[j], cos, sin, need_ctx)
        x = layer_norm(DEEPNORM_ALPHA * x + gate[:, None, :] * y, ln_g[i], ln_b[i])
        if need_ctx:
            xc = layer_norm(DEEPNORM_ALPHA * xc + gate_c * yc, ln_g[i], ln_b[i])
    return x


_drawn_inputs = setup_inputs


def setup_inputs(seed=0):
    import zlib

    import numpy as np

    out = dict(_drawn_inputs(seed))
    spreads = {}
    factors = {'ctx': 4.715,
     'c_ctx': 4.178,
     'ada_b': 7.358,
     'gdn_a_log': 7.108,
     'gdn_dt_bias': 4.657,
     'gdn_norm': 8.0,
     'rwkv_w0': 3.013,
     'rwkv_w1': 8.0,
     'rwkv_w2': 8.0,
     'rwkv_a0': 8.0,
     'rwkv_a1': 8.0,
     'rwkv_a2': 8.0,
     'rwkv_k_k': 8.0,
     'rwkv_k_a': 8.0,
     'rwkv_r_k': 4.205,
     'rwkv_gn_g': 8.0,
     'rwkv_gn_b': 8.0,
     'gla_w_g2': 5.279,
     'gla_norm': 8.0,
     'mla_w_in': 4.607,
     'mla_q_norm': 8.0,
     'mla_kv_norm': 8.0,
     'mla_w_uq': 8.0,
     'mla_w_ukv': 4.552,
     'mla_w_out': 4.471}
    for name, (base, spread) in spreads.items():
        noise = np.random.default_rng([zlib.crc32(name.encode()), seed]).standard_normal(out[name].shape)
        drawn = base * np.exp(spread * noise) if base else spread * noise
        out[name] = jnp.asarray(drawn.astype(out[name].dtype))
    for name, factor in factors.items():
        out[name] = (out[name] * factor).astype(out[name].dtype)
    return out
```

```python
import math
from contextlib import ExitStack

import numpy as np

import concourse.bass as bass
from concourse import mybir

F32 = mybir.dt.float32
U8 = mybir.dt.uint8
ALU = mybir.AluOpType
ACT = mybir.ActivationFunctionType
AX = mybir.AxisListType

P = 128
D = 1024
KC = D // P
TX, TC = 1024, 256
T = TC + TX
NT = T // P
DEPTH = 4
ALPHA = (2.0 * DEPTH) ** 0.25
LEVELS = 7
GC = 64
SPANS = ((TC, 512), (TC + 512, 512), (0, TC))


class Stage:

    def __init__(self, nc):
        self.nc, self.stack, self.sems = nc, ExitStack(), []

    def __enter__(self):
        self.inner = ExitStack()
        return self

    def __exit__(self, *exc):
        self.inner.close()
        if exc[0] is None:
            with self.nc.Block() as block:
                sems = self.sems

                @block.sync
                def _(sp):
                    for s in sems:
                        sp.sem_clear(s)
        self.stack.close()
        return False

    def sb(self, name, shape, dtype=F32):
        return self.stack.enter_context(self.nc.sbuf_tensor(unique(name), shape, dtype))

    def ps(self, name, shape):
        return self.stack.enter_context(self.nc.psum_tensor(unique(name), shape, F32))

    def sem(self, name):
        s = self.stack.enter_context(self.nc.semaphore(unique(name)))
        self.sems.append(s)
        return s

    def block(self):
        return self.inner.enter_context(self.nc.Block())


NAMES = {}


def unique(name):
    NAMES[name] = NAMES.get(name, 0) + 1
    return f"{name}_{NAMES[name]}"


class Steps:

    def __init__(self, eng, sem, it=0, per=0, first=0):
        self.eng, self.sem, self.it, self.per, self.first, self.n = eng, sem, it, per, first, 0

    def go(self, ins):
        self.n += 1
        ins.then_inc(self.sem, 1)

    def __call__(self, ins):
        self.go(ins)
        self.eng.wait_ge(self.sem, self.it * self.per + (self.first + self.n))

    def done(self):
        assert self.n == self.per, (self.n, self.per)


def product(nc, out, weights, moving, spans=SPANS):
    for bank, (t0, n) in enumerate(spans):
        kcs = moving.shape[1]
        for kc in range(kcs):
            last = nc.tensor.matmul(out[:, bank, 0:n], weights[:, kc, :], moving[:, kc, t0:t0 + n],
                                    start=kc == 0, stop=kc == kcs - 1)
    return last


def block_of(w, i, n=P):
    return w.rearrange("(k p) c -> p k c", p=P)[:, :, bass.ds(i * n, n)]


def load_constants(nc, a, R):
    with Stage(nc) as st:
        loaded, kept = st.sem("constants_loaded"), st.sem("masks_kept")
        masks = {"join_masks": st.sb("join_masks_in", [P, 2 * LEVELS, P]), "mask64": st.sb("mask64_in", [GC, 2, GC])}
        block = st.block()

        @block.sync
        def _(sp):
            names = ("ident", "ones", "off", "strict", "incl", "head_ones", "swap")
            for n in names:
                sp.dma_start(R[n][:], a["c_" + n]).then_inc(loaded, 16)
            for n, m in masks.items():
                sp.dma_start(m[:, :, :], a["c_" + n]).then_inc(loaded, 16)

        @block.vector
        def _(dve):
            dve.wait_ge(loaded, 16 * 9)
            for n, m in masks.items():
                nc.vector.tensor_copy(R[n][:, :, :], m[:, :, :]).then_inc(kept, 1)


def modulation(nc, a, R, S):
    G = 6
    N = 3 * D // G
    with Stage(nc) as st:
        cs = st.sb("cond", [P, KC, 2])
        sg = st.sb("cond_sigmoid", [P, KC, 2])
        w = [st.sb("ada_slot", [P, KC, N]) for _ in range(2)]
        b = [st.sb("ada_bias", [2, N]) for _ in range(2)]
        o = [st.sb("mods_out", [2, N]) for _ in range(2)]
        ps = [st.ps("mods_ps", [P, 512]) for _ in range(2)]
        c_in = st.sem("cond_loaded")
        sig = st.sem("sigmoid_ready")
        silu = st.sem("silu_ready")
        w_in = [st.sem("ada_loaded") for _ in range(2)]
        mm = st.sem("product_ready")
        row = st.sem("row_ready")
        out = [st.sem("mods_stored") for _ in range(2)]
        block = st.block()

        @block.sync
        def _(sp):
            with nc.allow_non_contiguous_dma("8 values a partition"):
                sp.dma_start(cs[:, :, 0], a["c"].rearrange("o (p k) -> (o p) k", k=KC)).then_inc(c_in, 16)
                sp.dma_start(cs[:, :, 1], a["c_ctx"].rearrange("(p k) -> p k", k=KC)).then_inc(c_in, 16)
            with sp.Fori(0, DEPTH) as l:
                for g in range(G):
                    s = g % 2
                    sp.wait_ge(row, l * G + g + 1)
                    wl = a["ada_w"][bass.ds(l, 1), :, g * N:(g + 1) * N].rearrange("o (p k) n -> p (o k) n", k=KC)
                    sp.dma_start(w[s][:, :, :], wl).then_inc(w_in[s], 16)
                    bl = a["ada_b"][bass.ds(l, 1), g * N:(g + 1) * N]
                    sp.dma_start(b[s][:, :], bl.to_broadcast([2, N])).then_inc(w_in[s], 16)

        @block.scalar
        def _(act):
            for s in range(2):
                act.sem_inc(out[s], 16)
            act.wait_ge(c_in, 32)
            nc.scalar.activation(sg[:, :, :], cs[:, :, :], ACT.Sigmoid).then_inc(sig, 1)
            with act.Fori(0, DEPTH) as l:
                for g in range(G):
                    s = g % 2
                    dst = S["mods"][:, bass.ds(l, 1), g * N:(g + 1) * N].rearrange("s o n -> s (o n)")
                    act.wait_ge(row, l * G + g + 3)
                    act.dma_start(dst, o[s][:, :]).then_inc(out[s], 16)
            for s in range(2):
                act.wait_ge(out[s], 16 * (DEPTH * G // 2 + 1))

        @block.vector
        def _(dve):
            dve.sem_inc(row, 2)
            dve.wait_ge(sig, 1)
            nc.vector.tensor_tensor(cs[:, :, :], cs[:, :, :], sg[:, :, :], ALU.mult).then_inc(silu, 1)
            with dve.Fori(0, DEPTH) as l:
                for g in range(G):
                    s = g % 2
                    dve.wait_ge(w_in[s], (l * (G // 2) + g // 2 + 1) * 32)
                    dve.wait_ge(out[s], (l * (G // 2) + g // 2 + 1) * 16)
                    dve.wait_ge(mm, l * G + g + 1)
                    add = 1.0 if g in (2, 3) else 0.0
                    nc.vector.scalar_tensor_tensor(out=o[s][:, :], in0=ps[s][0:2, 0:N], scalar=add, in1=b[s][:, :],
                                                   op0=ALU.add, op1=ALU.add).then_inc(row, 1)

        @block.tensor
        def _(pe):
            pe.wait_ge(silu, 1)
            with pe.Fori(0, DEPTH) as l:
                for g in range(G):
                    s = g % 2
                    pe.wait_ge(w_in[s], (l * (G // 2) + g // 2 + 1) * 32)
                    pe.wait_ge(row, l * G + g + 1)
                    for kc in range(KC):
                        last = nc.tensor.matmul(ps[s][0:2, 0:N], cs[:, kc, :], w[s][:, kc, :],
                                                start=kc == 0, stop=kc == KC - 1)
                    last.then_inc(mm, 1)


def turn_in(nc, a, R):
    with Stage(nc) as st:
        rows = [st.sb("token_rows", [P, D]) for _ in range(2)]
        ps = [st.ps("turned", [P, KC, P]) for _ in range(2)]
        rows_in = [st.sem("rows_loaded") for _ in range(2)]
        turned = st.sem("turned_ready")
        kept = st.sem("tile_kept")
        block = st.block()

        @block.sync
        def _(sp):
            for t in range(NT):
                src = a["ctx"][0, t * P:(t + 1) * P, :] if t < TC // P else a["x"][0, t * P - TC:(t + 1) * P - TC, :]
                sp.wait_ge(kept, t + 1)
                sp.dma_start(rows[t % 2][:, :], src).then_inc(rows_in[t % 2], 16)

        @block.tensor
        def _(pe):
            for t in range(NT):
                pe.wait_ge(rows_in[t % 2], 16 * (t // 2 + 1))
                pe.wait_ge(kept, t + 1)
                for kc in range(KC):
                    last = nc.tensor.transpose(ps[t % 2][:, kc, :], rows[t % 2][:, kc * P:(kc + 1) * P], R["ident"][:, :])
                last.then_inc(turned, 1)

        @block.vector
        def _(dve):
            dve.sem_inc(kept, 2)
            for t in range(NT):
                dve.wait_ge(turned, t + 1)
                nc.vector.tensor_copy(R["xT"][:, :, t * P:(t + 1) * P], ps[t % 2][:, :, :]).then_inc(kept, 1)


def modulate(nc, a, R, S, layer):
    with Stage(nc) as st:
        m = R["mod"]
        loaded = st.sem("mods_loaded")
        h_ready = st.sem("h_ready")
        block = st.block()

        @block.sync
        def _(sp):
            with nc.allow_non_contiguous_dma("24 values a partition"):
                for s in range(2):
                    sp.dma_start(m[:, s, :], S["mods"][s, layer, :].rearrange("(j p) -> p j", p=P)).then_inc(loaded, 16)
                sp.dma_start(R["ln"][:, 0, :], a["ln_g"][layer, :].rearrange("(j p) -> p j", p=P)).then_inc(loaded, 16)
                sp.dma_start(R["ln"][:, 1, :], a["ln_b"][layer, :].rearrange("(j p) -> p j", p=P)).then_inc(loaded, 16)
            sp.wait_ge(loaded, 64)

        def spans(kc):
            for s, t0, n in ((1, 0, TC), (0, TC, TX)):
                yield R["hT"][:, kc, t0:t0 + n], R["xT"][:, kc, t0:t0 + n], m[:, s, kc:kc + 1], m[:, s, KC + kc:KC + kc + 1]

        @block.vector
        def _(dve):
            dve.wait_ge(loaded, 64)
            for kc in range(0, KC, 2):
                for h, x, shift, scale in spans(kc):
                    nc.vector.tensor_scalar(h, x, scale, shift, ALU.mult, ALU.add).then_inc(h_ready, 1)

        @block.scalar
        def _(act):
            act.wait_ge(loaded, 64)
            for kc in range(1, KC, 2):
                for h, x, shift, scale in spans(kc):
                    nc.scalar.activation(h, x, ACT.Identity, bias=shift, scale=scale).then_inc(h_ready, 1)


def put_out(nc, a, R, w_out, layer, need_ctx):
    with Stage(nc) as st:
        m, ln, xT = R["mod"], R["ln"], R["xT"]
        w = [st.sb("w_out_slot", [P, KC, P]) for _ in range(2)]
        gy = [st.sb("gated_y", [P, T]) for _ in range(2)]
        sq = [st.sb("squares", [P, T]) for _ in range(2)]
        mean = st.sb("mean", [P, T])
        rstd = st.sb("rstd", [P, T])
        ps = [st.ps("y_ps", [P, 3, 512]) for _ in range(2)]
        w_in = [st.sem("w_loaded") for _ in range(2)]
        mm = st.sem("y_ready")
        gated = st.sem("gated_ready")
        summed = st.sem("x_summed")
        mean_ps, mean_sb = st.sem("mean_in_psum"), st.sem("mean_kept")
        centred, squared, var_ps = st.sem("centred"), st.sem("squared"), st.sem("square_sum_ready")
        root, inv, scaled, done = st.sem("root_ready"), st.sem("rstd_ready"), st.sem("scaled"), st.sem("normed")
        block = st.block()
        parts = ((0, 0, 2, TC, TX), (1, 2, 1, 0, TC))

        def psum_part(tile, bank, banks):
            return tile[:, bank:bank + banks, :].rearrange("p b n -> p (b n)") if banks > 1 else tile[:, bank, 0:TC]

        @block.sync
        def _(sp):
            for c in range(KC):
                if c >= 2:
                    sp.wait_ge(mm, c - 1)
                sp.dma_start(w[c % 2][:, :, :], block_of(w_out, c)).then_inc(w_in[c % 2], 16)

        @block.tensor
        def _(pe):
            for c in range(KC):
                pe.wait_ge(w_in[c % 2], 16 * (c // 2 + 1))
                if c >= 2:
                    pe.wait_ge(gated, 2 * (c - 1))
                product(nc, ps[c % 2], w[c % 2], R["hT"]).then_inc(mm, 1)
            pe.wait_ge(summed, KC)
            pe.wait_ge(gated, 2 * KC)
            product(nc, ps[0], ones_of(R), xT).then_inc(mean_ps, 1)
            for c in range(KC):
                pe.wait_ge(squared, c + 1)
                for bank, (t0, n) in enumerate(SPANS):
                    last = nc.tensor.matmul(ps[1][:, bank, 0:n], R["ones"][:, :], sq[c % 2][:, t0:t0 + n],
                                            start=c == 0, stop=c == KC - 1)
                last.then_inc(var_ps, 1)

        @block.scalar
        def _(act):
            for c in range(KC):
                act.wait_ge(mm, c + 1)
                if c >= 2:
                    act.wait_ge(summed, c - 1)
                for s, bank, banks, t0, n in parts:
                    nc.scalar.activation(gy[c % 2][:, t0:t0 + n], psum_part(ps[c % 2], bank, banks), ACT.Identity,
                                         scale=m[:, s, 2 * KC + c:2 * KC + c + 1]).then_inc(gated, 1)
            for c in range(KC):
                act.wait_ge(centred, c + 1)
                if c >= 2:
                    act.wait_ge(var_ps, c - 1)
                nc.scalar.activation(sq[c % 2][:, :], xT[:, c, :], ACT.Square).then_inc(squared, 1)
            act.wait_ge(var_ps, KC)
            act.wait_ge(root, 1)
            nc.scalar.activation(rstd[:, :], rstd[:, :], ACT.Sqrt).then_inc(root, 1)
            for c in range(KC):
                act.wait_ge(scaled, c + 1)
                nc.scalar.activation(xT[:, c, :], xT[:, c, :], ACT.Identity, bias=ln[:, 1, c:c + 1],
                                     scale=ln[:, 0, c:c + 1]).then_inc(done, 1)

        @block.vector
        def _(dve):
            for c in range(KC):
                dve.wait_ge(gated, 2 * (c + 1))
                nc.vector.scalar_tensor_tensor(out=xT[:, c, :], in0=xT[:, c, :], scalar=ALPHA, in1=gy[c % 2][:, :],
                                               op0=ALU.mult, op1=ALU.add).then_inc(summed, 1)
            dve.wait_ge(mean_ps, 1)
            for s, bank, banks, t0, n in parts:
                nc.vector.tensor_scalar(mean[:, t0:t0 + n], psum_part(ps[0], bank, banks), 1.0 / D, None,
                                        ALU.mult).then_inc(mean_sb, 1)
            dve.wait_ge(mean_sb, 2)
            for c in range(KC):
                nc.vector.tensor_tensor(xT[:, c, :], xT[:, c, :], mean[:, :], ALU.subtract).then_inc(centred, 1)
            dve.wait_ge(var_ps, KC)
            for i, (s, bank, banks, t0, n) in enumerate(parts):
                ins = nc.vector.tensor_scalar(rstd[:, t0:t0 + n], psum_part(ps[1], bank, banks), 1.0 / D, 1e-5,
                                              ALU.mult, ALU.add)
            ins.then_inc(root, 1)
            dve.wait_ge(root, 2)
            nc.vector.reciprocal(rstd[:, :], rstd[:, :]).then_inc(inv, 1)
            dve.wait_ge(inv, 1)
            for c in range(KC):
                nc.vector.tensor_tensor(xT[:, c, :], xT[:, c, :], rstd[:, :], ALU.mult).then_inc(scaled, 1)


def ones_of(R):
    return R["ones"][:, :].rearrange("p (o n) -> p o n", o=1).to_broadcast([P, KC, P])


def turn_out(nc, R, out):
    with Stage(nc) as st:
        rows = [st.sb("token_rows", [P, D]) for _ in range(2)]
        ps = [st.ps("turned", [P, KC, P]) for _ in range(2)]
        turned, kept = st.sem("turned_ready"), st.sem("rows_kept")
        stored = [st.sem("rows_stored") for _ in range(2)]
        block = st.block()
        n = TX // P

        @block.tensor
        def _(pe):
            for t in range(n):
                if t >= 2:
                    pe.wait_ge(kept, t - 1)
                for kc in range(KC):
                    last = nc.tensor.transpose(ps[t % 2][:, kc, :], R["xT"][:, kc, TC + t * P:TC + (t + 1) * P], R["ident"][:, :])
                last.then_inc(turned, 1)

        @block.vector
        def _(dve):
            for t in range(n):
                dve.wait_ge(turned, t + 1)
                if t >= 2:
                    dve.wait_ge(stored[t % 2], 16 * (t // 2))
                nc.vector.tensor_copy(rows[t % 2][:, :], ps[t % 2][:, :, :].rearrange("p k n -> p (k n)")).then_inc(kept, 1)

        @block.sync
        def _(sp):
            for t in range(n):
                sp.wait_ge(kept, t + 1)
                sp.dma_start(out[0, t * P:(t + 1) * P, :], rows[t % 2][:, :]).then_inc(stored[t % 2], 16)
            for s in range(2):
                sp.wait_ge(stored[s], 16 * n // 2)


def f32(bits):
    return float(np.frombuffer(bytes.fromhex(bits)[::-1], np.float64)[0])


EXP_MIN, EXP_MAX = f32("C055F33340000000"), f32("4056333340000000")
LOG2E, LN2_HIGH, LN2_LOW = f32("3FF7154760000000"), f32("3FE6300000000000"), f32("BF2BD01060000000")
EXP = [f32(b) for b in ("3F2A0D2CE0000000", "3F56E879C0000000", "3F81112100000000", "3FA5553820000000", "3FC5555540000000",
                        "3FE0000000000000")]
LOG = [[f32(b) for b in row] for row in (("3FB2043760000000", "BFBD7A3700000000", "3FBDE4A340000000"),
                                         ("BFBFCBA9E0000000", "3FC23D37E0000000", "BFC555CA00000000"),
                                         ("3FC999D580000000", "BFCFFFFF80000000", "3FD5555540000000"))]
LOG1P_BELOW = [f32(b) for b in ("3FF0000000000000", "402E2035A0000000", "4054C30B60000000", "406BB865A0000000",
                                "4073519460000000", "406B0DB140000000", "404E0F3040000000")]
LOG1P_ABOVE = [f32(b) for b in ("3F07BC0960000000", "3FDFE818A0000000", "401A509F40000000", "403DE97380000000",
                                "404E798EC0000000", "404C8E75A0000000", "40340A2020000000")]
LOG1P_SMALL, ROOT_HALF = f32("3FDA8279A0000000"), f32("3FE6A09E60000000")
HALVER = 4097.0
TO_INTEGER = 1.5 * 2.0 ** 23


def add_rounded(V, step, out, c, p, e, s, b, d, q):
    step(V.tensor_tensor(s, c, p, ALU.add))
    step(V.tensor_tensor(b, s, c, ALU.subtract))
    step.go(V.tensor_tensor(d, s, b, ALU.subtract))
    step(V.tensor_tensor(q, p, b, ALU.subtract))
    step(V.tensor_tensor(d, c, d, ALU.subtract))
    step(V.tensor_tensor(d, d, q, ALU.add))
    step(V.tensor_tensor(d, d, e, ALU.add))
    step(V.tensor_tensor(out, s, d, ALU.add))


class Fused:

    def __init__(self, nc, st, shape, view):
        self.V, self.view = nc.vector, view
        self.p, self.e, self.s, self.b, self.d, self.q, self.m = (self.tile(st, n, shape) for n in (
            "product", "product_error", "sum", "sum_part", "sum_error", "sum_rest", "partial"))
        self.x_halves, self.y_halves = ([self.tile(st, n, shape) for n in ("high_half", "low_half")] for _ in range(2))

    def tile(self, st, name, shape):
        return self.view(st.sb(name, shape))

    def split(self, step, x, halves):
        V, (high, low) = self.V, halves
        step(V.scalar_tensor_tensor(out=low, in0=x, scalar=HALVER, in1=x, op0=ALU.mult, op1=ALU.subtract))
        step(V.scalar_tensor_tensor(out=high, in0=x, scalar=HALVER, in1=low, op0=ALU.mult, op1=ALU.subtract))
        step(V.tensor_tensor(low, x, high, ALU.subtract))
        return halves

    def product(self, step, x, y, y_halves=None):
        V, p, e, m = self.V, self.p, self.e, self.m
        xh, xl = self.split(step, x, self.x_halves)
        if isinstance(y, float):
            c = np.float32(y) * np.float32(HALVER)
            yh = float(c - (c - np.float32(y)))
            yl = float(np.float32(y) - np.float32(yh))
            step(V.tensor_scalar(p, x, y, None, ALU.mult))
            step(V.scalar_tensor_tensor(out=e, in0=xh, scalar=yh, in1=p, op0=ALU.mult, op1=ALU.subtract))
            for half, number in ((xh, yl), (xl, yh), (xl, yl)):
                if number:
                    step(V.scalar_tensor_tensor(out=e, in0=half, scalar=number, in1=e, op0=ALU.mult, op1=ALU.add))
            return
        yh, yl = y_halves or self.split(step, y, self.y_halves)
        step(V.tensor_tensor(p, x, y, ALU.mult))
        step(V.tensor_tensor(e, xh, yh, ALU.mult))
        step(V.tensor_tensor(e, e, p, ALU.subtract))
        for a, b in ((xh, yl), (xl, yh), (xl, yl)):
            step(V.tensor_tensor(m, a, b, ALU.mult))
            step(V.tensor_tensor(e, e, m, ALU.add))

    def fma(self, step, out, x, y, c, y_halves=None):
        V, s, b, d, q = self.V, self.s, self.b, self.d, self.q
        self.product(step, x, y, y_halves)
        if not isinstance(c, float):
            return add_rounded(V, step, out, c, self.p, self.e, s, b, d, q)
        step(V.tensor_scalar(s, self.p, c, None, ALU.add))
        step(V.tensor_scalar(b, s, c, None, ALU.subtract))
        step.go(V.tensor_tensor(d, s, b, ALU.subtract))
        step(V.tensor_tensor(q, self.p, b, ALU.subtract))
        step(V.tensor_scalar(d, d, -1.0, c, ALU.mult, ALU.add))
        step(V.tensor_tensor(d, d, q, ALU.add))
        step(V.tensor_tensor(d, d, self.e, ALU.add))
        step(V.tensor_tensor(out, s, d, ALU.add))

    def divide(self, step, out, x, y, inverse):
        V = self.V
        step(V.reciprocal(inverse, y))
        step(V.tensor_tensor(out, x, inverse, ALU.mult))
        self.product(step, out, y)
        step(V.tensor_tensor(self.d, x, self.p, ALU.subtract))
        step(V.tensor_tensor(self.d, self.d, self.e, ALU.subtract))
        step(V.tensor_tensor(self.d, self.d, inverse, ALU.mult))
        step(V.tensor_tensor(out, out, self.d, ALU.add))

    def exp(self, step, x, n, y, z, whole):
        V = self.V
        step(V.tensor_scalar(x, x, EXP_MIN, EXP_MAX, ALU.max, ALU.min))
        self.fma(step, y, x, LOG2E, 0.5)
        step(V.tensor_scalar(n, y, TO_INTEGER, TO_INTEGER, ALU.add, ALU.subtract))
        step(V.tensor_tensor(z, n, y, ALU.is_gt))
        step(V.tensor_tensor(n, n, z, ALU.subtract))
        step(V.tensor_scalar(n, n, -127.0, 127.0, ALU.max, ALU.min))
        self.fma(step, x, n, -LN2_HIGH, x)
        self.fma(step, x, n, -LN2_LOW, x)
        self.fma(step, y, x, EXP[0], EXP[1])
        halves = self.split(step, x, self.y_halves)
        for c in EXP[2:]:
            self.fma(step, y, y, x, c, halves)
        step(V.tensor_tensor(z, x, x, ALU.mult))
        self.fma(step, y, y, z, x)
        step(V.tensor_scalar(y, y, 1.0, None, ALU.add))
        step(V.tensor_scalar(n, n, 127.0, 2.0 ** 23, ALU.add, ALU.mult))
        step(V.tensor_copy(whole, n))
        step(V.tensor_tensor(y, y, whole.bitcast(F32), ALU.mult))

    def log1p(self, step, u, out, t):
        V = self.V
        y, two, m, low, x2, x3, a = t
        step(V.tensor_scalar(y, u, 1.0, None, ALU.add))
        step(V.tensor_scalar(two, y, 2.0, None, ALU.is_ge))
        step(V.tensor_scalar(m, two, -0.25, 0.5, ALU.mult, ALU.add))
        step(V.tensor_tensor(m, m, y, ALU.mult))
        step(V.tensor_scalar(low, m, ROOT_HALF, None, ALU.is_lt))
        step(V.tensor_tensor(y, m, low, ALU.mult))
        step(V.scalar_tensor_tensor(out=m, in0=m, scalar=1.0, in1=y, op0=ALU.subtract, op1=ALU.add))
        step(V.scalar_tensor_tensor(out=low, in0=two, scalar=1.0, in1=low, op0=ALU.add, op1=ALU.subtract))
        step(V.tensor_tensor(x2, m, m, ALU.mult))
        step(V.tensor_tensor(x3, x2, m, ALU.mult))
        for i, (c0, c1, c2) in enumerate(LOG):
            part = (out, y, a)[i]
            self.fma(step, part, m, c0, c1)
            self.fma(step, part, part, m, c2)
        self.fma(step, y, out, x3, y)
        self.fma(step, a, y, x3, a)
        step(V.tensor_scalar(y, low, LN2_LOW, None, ALU.mult))
        self.fma(step, a, a, x3, y)
        self.fma(step, y, x2, -0.5, m)
        step(V.tensor_tensor(y, y, a, ALU.add))
        self.fma(step, out, low, LN2_HIGH, y)
        halves = self.split(step, u, self.y_halves)
        for part, coefficients in ((m, LOG1P_BELOW), (low, LOG1P_ABOVE)):
            step(V.memset(part, coefficients[0]))
            for c in coefficients[1:]:
                self.fma(step, part, part, u, c, halves)
        self.divide(step, y, low, m, a)
        step(V.tensor_tensor(x2, u, u, ALU.mult))
        step(V.tensor_tensor(x3, u, x2, ALU.mult))
        step(V.tensor_tensor(y, x3, y, ALU.mult))
        self.fma(step, y, x2, -0.5, y)
        step(V.tensor_tensor(y, u, y, ALU.add))
        step(V.scalar_tensor_tensor(out=y, in0=u, scalar=LOG1P_SMALL, in1=y, op0=ALU.is_lt, op1=ALU.mult))
        step(V.scalar_tensor_tensor(out=out, in0=u, scalar=LOG1P_SMALL, in1=out, op0=ALU.is_ge, op1=ALU.mult))
        step(V.tensor_tensor(out, out, y, ALU.add))


def context_silu(nc, a, S):
    with Stage(nc) as st:
        view = lambda t: t[:, :]
        F = Fused(nc, st, [P, KC], view)
        x, u, n, y, z, one = (view(st.sb(name, [P, KC])) for name in ("c_ctx", "minus_c", "n", "exp", "scratch", "one"))
        whole = st.sb("whole", [P, KC], mybir.dt.int32)
        loaded, step_s, ready, stored = st.sem("c_loaded"), st.sem("vector_step"), st.sem("silu_ready"), st.sem("silu_stored")
        block = st.block()

        @block.sync
        def _(sp):
            sp.dma_start(x, a["c_ctx"].rearrange("(p k) -> p k", k=KC)).then_inc(loaded, 16)
            sp.wait_ge(ready, 1)
            sp.dma_start(S["silu_ctx"].rearrange("(p k) -> p k", k=KC), z).then_inc(stored, 16)
            sp.wait_ge(stored, 16)

        @block.vector
        def _(dve):
            V, step = nc.vector, Steps(dve, step_s)
            dve.wait_ge(loaded, 16)
            step(V.memset(one, 1.0))
            step(V.tensor_scalar(u, x, -1.0, None, ALU.mult))
            F.exp(step, u, n, y, z, whole[:, :])
            step(V.tensor_scalar(y, y, 1.0, None, ALU.add))
            F.divide(step, z, one, y, n)
            V.tensor_tensor(z, x, z, ALU.mult).then_inc(ready, 1)


def products_with_errors(V, step, x, x_halves, y, y_halves, p, e, m):
    (xh, xl), (yh, yl) = x_halves, y_halves
    step(V.tensor_tensor(p, x, y, ALU.mult))
    step(V.tensor_tensor(e, xh, yh, ALU.mult))
    step(V.tensor_tensor(e, e, p, ALU.subtract))
    for a, b in ((xh, yl), (xl, yh), (xl, yl)):
        step(V.tensor_tensor(m, a, b, ALU.mult))
        step(V.tensor_tensor(e, e, m, ALU.add))


def halve(V, step, x, high, low):
    step(V.tensor_scalar(high, x, HALVER, None, ALU.mult))
    step(V.tensor_tensor(low, high, x, ALU.subtract))
    step(V.tensor_tensor(high, high, low, ALU.subtract))
    step(V.tensor_tensor(low, x, high, ALU.subtract))


UNROLL = 32
ADD = 8
SPLIT, PRODUCTS = 4, 9


def context_modulation(nc, a, R, S):
    C = 2 * KC
    J = P // UNROLL
    with Stage(nc) as st:
        rows = [st.sb("ada_rows", [P, C * P]) for _ in range(2)]
        wT = [st.sb("ada_columns", [P, C, P]) for _ in range(2)]
        wh, wl, m = (st.sb(n, [P, C, P]) for n in ("w_high", "w_low", "partial"))
        c, ch, cl = (st.sb(n, [P, D]) for n in ("silu_c", "c_high", "c_low"))
        p, e = ([st.sb(n, [P, C, P]) for _ in range(2)] for n in ("products", "errors"))
        acc, s, b, d, q = (st.sb(n, [P, C]) for n in ("chain", "sum", "sum_part", "sum_error", "sum_rest"))
        now = [st.sb(n, [P, C, UNROLL]) for n in ("products_now", "errors_now")]
        bias, tick = st.sb("ada_bias", [P, C]), st.sb("tick", [1, 1])
        ps = [st.ps("turned_ps", [P, C, P]) for _ in range(2)]
        small_in, rows_in = st.sem("small_loaded"), [st.sem("rows_loaded") for _ in range(2)]
        turned, kept = st.sem("rows_turned"), st.sem("columns_kept")
        split_s, pool_s, step_s, done = st.sem("c_split"), st.sem("pool_step"), st.sem("chain_step"), st.sem("modulation_done")
        block = st.block()
        N = D // P
        PER = J * (2 + UNROLL * ADD)
        POOL = SPLIT + PRODUCTS

        @block.sync
        def _(sp):
            sp.dma_start(c[:, :], S["silu_ctx"].rearrange("(o c) -> o c", o=1).to_broadcast([P, D])).then_inc(small_in, 16)
            with nc.allow_non_contiguous_dma("16 values a partition"):
                sp.dma_start(bias[:, :], a["ada_b"][0, 0:2 * D].rearrange("(c p) -> p c", p=P)).then_inc(small_in, 16)
            for i in range(N):
                if i >= 2:
                    sp.wait_ge(turned, i - 1 + 2)
                sp.dma_start(rows[i % 2][:, :], a["ada_w"][0, i * P:(i + 1) * P, 0:2 * D]).then_inc(rows_in[i % 2], 16)

        @block.tensor
        def _(pe):
            pe.sem_inc(turned, 2)
            for i in range(N):
                pe.wait_ge(rows_in[i % 2], 16 * (i // 2 + 1))
                pe.wait_ge(kept, i + 1)
                for j in range(C):
                    last = nc.tensor.transpose(ps[i % 2][:, j, :], rows[i % 2][:, j * P:(j + 1) * P], R["ident"][:, :])
                last.then_inc(turned, 1)

        @block.scalar
        def _(act):
            act.sem_inc(kept, 2)
            for i in range(N):
                act.wait_ge(turned, i + 1 + 2)
                if i >= 2:
                    act.wait_ge(pool_s, (i - 1) * POOL)
                nc.scalar.copy(wT[i % 2][:, :, :], ps[i % 2][:, :, :]).then_inc(kept, 1)

        @block.gpsimd
        def _(pool):
            G = nc.gpsimd
            pool.wait_ge(small_in, 32)
            halve(G, Steps(pool, split_s), c[:, :], ch[:, :], cl[:, :])
            step = Steps(pool, pool_s)
            for i in range(N):
                k = slice(i * P, (i + 1) * P)
                wide = lambda t: t[:, k].rearrange("p (o k) -> p o k", o=1).to_broadcast([P, C, P])
                pool.wait_ge(kept, i + 1 + 2)
                halve(G, step, wT[i % 2][:, :, :], wh[:, :, :], wl[:, :, :])
                if i >= 2:
                    pool.wait_ge(step_s, (i - 1) * PER + 1)
                products_with_errors(G, step, wT[i % 2][:, :, :], (wh[:, :, :], wl[:, :, :]), wide(c), (wide(ch), wide(cl)),
                                     p[i % 2][:, :, :], e[i % 2][:, :, :], m[:, :, :])

        @block.vector
        def _(dve):
            V = nc.vector
            V.memset(acc[:, :], 0.0).then_inc(step_s, 1)
            dve.wait_ge(step_s, 1)
            with dve.Fori(0, N // 2) as it:
                for slot in range(2):
                    dve.wait_ge(pool_s, (it * 2 + slot + 1) * POOL)
                    V.memset(tick[:, :], 0.0)
                    with dve.Fori(0, J) as j:
                        step = Steps(dve, step_s, (it * 2 + slot) * J + j, 2 + UNROLL * ADD, first=1)
                        step.go(V.tensor_copy(now[0][:, :, :], p[slot][:, :, bass.ds(j * UNROLL, UNROLL)]))
                        step(V.tensor_copy(now[1][:, :, :], e[slot][:, :, bass.ds(j * UNROLL, UNROLL)]))
                        for u in range(UNROLL):
                            add_rounded(V, step, acc[:, :], acc[:, :], now[0][:, :, u], now[1][:, :, u], s[:, :], b[:, :], d[:, :], q[:, :])
                        step.done()
            dve.wait_ge(small_in, 32)
            V.tensor_tensor(R["mod_ctx"][:, :, :].rearrange("p n c -> p (n c)"), acc[:, :], bias[:, :], ALU.add).then_inc(done, 1)
            dve.wait_ge(done, 1)
            V.tensor_scalar(R["mod_ctx"][:, 1, :], R["mod_ctx"][:, 1, :], 1.0, None, ALU.add).then_inc(done, 1)


PIECE = 32
PIECES = D // PIECE


class ContextLogits:

    CT, N = TC // P, 2 * 8
    STEPS = PIECE // 2 * ADD
    PRODUCTS = SPLIT + PRODUCTS

    def __init__(self, nc, es, a, R, S):
        self.nc, self.R, self.S = nc, R, S
        sb = lambda name, *shape: es.enter_context(nc.sbuf_tensor(unique(name), [P, *shape], F32))
        CT, N = self.CT, self.N
        self.h, self.hh, self.hl = (sb(n, CT, D) for n in ("h_ctx", "h_high", "h_low"))
        self.w = [sb("gate_w", PIECE, N) for _ in range(2)]
        self.wh, self.wl, self.m = sb("gate_w_high", PIECE, N), sb("gate_w_low", PIECE, N), sb("partial", CT, PIECE, N)
        self.p, self.e = ([sb(n, CT, PIECE, N) for _ in range(2)] for n in ("products", "errors"))
        self.scratch = [sb(n, CT, 2 * N) for n in ("sum", "sum_part", "sum_error", "sum_rest")]
        self.piece = 0
        self.prepare(a)

    def prepare(self, a):
        nc, R, h = self.nc, self.R, self.h
        with Stage(nc) as st:
            hc = st.sb("h_by_channel", [P, KC, TC])
            ps = [st.ps("turned_ps", [P, KC, P]) for _ in range(self.CT)]
            gathered, h_ready, turned, kept = (st.sem(n) for n in ("w_gathered", "h_ready", "h_turned", "h_kept"))
            step_s, zeroed = st.sem("vector_step"), st.sem("chains_zeroed")
            block = st.block()

            @block.sync
            def _(sp):
                with nc.allow_non_contiguous_dma("eight values a row"):
                    for dr in range(2):
                        at = 4 * D + dr * 16 + 8
                        sp.dma_start(self.S["gate_w"][:, dr * 8:dr * 8 + 8], a["gdn_w_in"][0][:, at:at + 8]).then_inc(gathered, 16)
                sp.wait_ge(gathered, 32)

            @block.tensor
            def _(pe):
                pe.wait_ge(h_ready, KC)
                for t in range(self.CT):
                    for kc in range(KC):
                        last = nc.tensor.transpose(ps[t][:, kc, :], hc[:, kc, t * P:(t + 1) * P], R["ident"][:, :])
                    last.then_inc(turned, 1)

            @block.scalar
            def _(act):
                for t in range(self.CT):
                    act.wait_ge(turned, t + 1)
                    nc.scalar.copy(h[:, t, :], ps[t][:, :, :].rearrange("p k n -> p (k n)")).then_inc(kept, 1)

            @block.vector
            def _(dve):
                V = nc.vector
                for kc in range(KC):
                    V.tensor_scalar(hc[:, kc, :], R["xT"][:, kc, 0:TC], R["mod_ctx"][:, 1, kc:kc + 1], R["mod_ctx"][:, 0, kc:kc + 1],
                                    ALU.mult, ALU.add).then_inc(h_ready, 1)
                V.memset(R["chains_ctx"][:, :, :], 0.0).then_inc(zeroed, 1)
                dve.wait_ge(kept, self.CT)
                halve(V, Steps(dve, step_s), h[:, :, :], self.hh[:, :, :], self.hl[:, :, :])

    def begin(self, st, pieces):
        self.first, self.piece = self.piece, self.piece + pieces
        self.w_in = [st.sem("gate_w_loaded") for _ in range(2)]
        self.made, self.chained = st.sem("products_made"), st.sem("chain_step")

    def load(self, sp, i, slot):
        n = PIECE * self.N
        at = (i + self.first) * n
        wide = self.S["gate_w"].rearrange("(o k) n -> o (k n)", o=1)[:, bass.ds(at, n)].to_broadcast([P, n])
        sp.wait_ge(self.made, (i + 1) * self.PRODUCTS)
        sp.dma_start(self.w[slot][:, :, :].rearrange("p k n -> p (k n)"), wide).then_inc(self.w_in[slot], 16)

    def products(self, pool, pieces):
        G, CT, N = self.nc.gpsimd, self.CT, self.N
        pool.sem_inc(self.made, 2 * self.PRODUCTS)
        for i in range(pieces):
            slot = i % 2
            step = Steps(pool, self.made, i + 2, self.PRODUCTS)
            k = slice((i + self.first) * PIECE, (i + self.first + 1) * PIECE)
            over = lambda t: t[:, :, k].rearrange("p t (k o) -> p t k o", o=1).to_broadcast([P, CT, PIECE, N])
            wide = lambda t: t[:, :, :].rearrange("p (o k) n -> p o k n", o=1).to_broadcast([P, CT, PIECE, N])
            full = lambda t: t[:, :, :, :]
            pool.wait_ge(self.w_in[slot], (i // 2 + 1) * 16)
            halve(G, step, self.w[slot][:, :, :], self.wh[:, :, :], self.wl[:, :, :])
            pool.wait_ge(self.chained, (i + 1) * self.STEPS)
            products_with_errors(G, step, wide(self.w[slot]), (wide(self.wh), wide(self.wl)), over(self.h), (over(self.hh), over(self.hl)),
                                 full(self.p[slot]), full(self.e[slot]), full(self.m))
            step.done()

    def chain_start(self, dve):
        dve.sem_inc(self.chained, 2 * self.STEPS)

    def chain(self, dve, it, slot):
        i = it * 2 + slot
        acc, sums = self.R["chains_ctx"][:, :, :], [t[:, :, :] for t in self.scratch]
        dve.wait_ge(self.made, (i + 3) * self.PRODUCTS)
        step = Steps(dve, self.chained, i + 2, self.STEPS)
        for u in range(PIECE // 2):
            at = lambda t: t[slot][:, :, 2 * u:2 * u + 2, :].rearrange("p t k n -> p t (k n)")
            add_rounded(self.nc.vector, step, acc, acc, at(self.p), at(self.e), *sums)
        step.done()


PAD = 2
TAPS = 2 * PAD + 1
WIDE = TC + TX + 2 * PAD
XAT = TC + 2 * PAD - PAD + PAD


def in_psum(tile, part):
    return tile[:, 2, 0:TC] if part else tile[:, 0:2, :].rearrange("p b n -> p (b n)")


def gdn_channels(nc, a, R, w, conv, heads, beside, norm=None, chan_out=None, tok_out=None):
    with Stage(nc) as st:
        w_sb = [st.sb("w_slot", [P, KC, P]) for _ in range(2)]
        cw = [st.sb("taps", [P, TAPS]) for _ in range(2)]
        pad = [st.sb("padded", [P, WIDE + 2 * PAD]) for _ in range(2)]
        cv = [st.sb("convolved", [P, WIDE]) for _ in range(2)]
        sg = [st.sb("sigmoid", [P, WIDE]) for _ in range(2)]
        nat = [st.sb("by_channel", [P, T]) for _ in range(2)]
        tok = [st.sb("by_token", [P, NT, P]) for _ in range(2)]
        rn = [st.sb("inverse_length", [P, NT]) for _ in range(2)]
        ps = [st.ps("product_ps", [P, 3, 512]) for _ in range(2)]
        small = [st.ps("length_ps", [P, NT]) for _ in range(2)]
        w_in = [st.sem("w_loaded") for _ in range(2)]
        zero = st.sem("pad_zeroed")
        mm = st.sem("product_ready")
        evac = st.sem("padded_ready")
        conv_d, sig, silu = st.sem("tap_done"), st.sem("sigmoid_ready"), st.sem("silu_ready")
        sqr, ssum, eps, root, inv, bc, nrm = (st.sem(n) for n in (
            "squared", "square_sum_ready", "eps_added", "root_ready", "inverse_ready", "spread_ready", "normed"))
        tr = st.sem("turned_ready")
        free = st.sem("psum_free")
        cst = [st.sem("channels_stored") for _ in range(2)]
        tst = [st.sem("tokens_stored") for _ in range(2)]
        beside.begin(st, heads)
        block = st.block()
        U = heads // 2

        @block.sync
        def _(sp):
            def load(it):
                for s in range(2):
                    src = block_of(w, it * 2 + s)
                    cs = conv[:, bass.ds((it * 2 + s) * P, P)].rearrange("t p -> p t")
                    sp.wait_ge(conv_d, (it * 2 + s + 1) * TAPS)
                    sp.wait_ge(mm, it * 2 + s + 1)
                    sp.dma_start(w_sb[s][:, :, :], src).then_inc(w_in[s], 16)
                    with nc.allow_non_contiguous_dma("five taps a channel"):
                        sp.dma_start(cw[s][:, :], cs).then_inc(w_in[s], 16)
                    beside.load(sp, it * 2 + s, s)

            def store(it):
                for s in range(2):
                    if chan_out is not None:
                        if tok_out is None:
                            sp.wait_ge(free, it * 2 + s + 3)
                        else:
                            sp.wait_ge(nrm, it * 2 + s + 1)
                        sp.dma_start(chan_out[bass.ds((it * 2 + s) * P, P), :], nat[s][:, :]).then_inc(cst[s], 16)
                    if tok_out is not None:
                        sp.wait_ge(free, it * 2 + s + 3)
                        sp.dma_start(tok_out.rearrange("(t p) c -> p t c", p=P)[:, :, bass.ds(it * (2 * P) + s * P, P)],
                                     tok[s][:, :, :]).then_inc(tst[s], 16)

            for s in range(2):
                sp.sem_inc(cst[s], 16)
                sp.sem_inc(tst[s], 16)
            load(0)
            with sp.Fori(0, U - 1) as it:
                load(it + 1)
                store(it)
            store(U - 1)
            for s in range(2):
                if chan_out is not None:
                    sp.wait_ge(cst[s], (U + 1) * 16)
                if tok_out is not None:
                    sp.wait_ge(tst[s], (U + 1) * 16)

        @block.tensor
        def _(pe):
            pe.sem_inc(mm, 2)
            with pe.Fori(0, U) as it:
                for s in range(2):
                    pe.wait_ge(w_in[s], (it + 1) * 32)
                    pe.wait_ge(free, it * 2 + s + 1)
                    product(nc, ps[s], w_sb[s], R["hT"]).then_inc(mm, 1)
                for s in range(2):
                    if norm:
                        pe.wait_ge(sqr, it * 2 + s + 1)
                        for t in range(NT):
                            last = nc.tensor.matmul(small[s][:, t:t + 1], sg[s][:, t * P:(t + 1) * P],
                                                    R["ones"][:, 0:1], start=True, stop=True)
                        last.then_inc(ssum, 1)
                        pe.wait_ge(inv, it * 2 + s + 1)
                        flat = ps[s][:, :, :].rearrange("p b n -> p (b n)")
                        for t in range(NT):
                            last = nc.tensor.matmul(flat[:, t * P:(t + 1) * P], rn[s][:, t:t + 1].to_broadcast([P, P]),
                                                    R["ident"][:, :], start=True, stop=True)
                        last.then_inc(bc, 1)
                    if tok_out is not None:
                        pe.wait_ge(nrm if norm else silu, (it * 2 + s + 1) * (1 if norm else 2))
                        flat = ps[s][:, :, :].rearrange("p b n -> p (b n)")
                        for t in range(NT):
                            last = nc.tensor.transpose(flat[:, t * P:(t + 1) * P], nat[s][:, t * P:(t + 1) * P],
                                                       R["ident"][:, :])
                        last.then_inc(tr, 1)

        @block.scalar
        def _(act):
            act.wait_ge(zero, 2)
            if tok_out is not None:
                act.sem_inc(free, 2)
            with act.Fori(0, U) as it:
                for s in range(2):
                    act.wait_ge(mm, it * 2 + s + 3)
                    nc.scalar.activation(pad[s][:, PAD:PAD + TC], in_psum(ps[s], 1), ACT.Identity).then_inc(evac, 1)
                    nc.scalar.activation(pad[s][:, XAT + PAD:XAT + PAD + TX], in_psum(ps[s], 0), ACT.Identity).then_inc(evac, 1)
                    act.wait_ge(conv_d, (it * 2 + s + 3) * TAPS)
                    nc.scalar.activation(sg[s][:, :], cv[s][:, :], ACT.Sigmoid).then_inc(sig, 1)
                for s in range(2):
                    if norm:
                        act.wait_ge(silu, (it * 2 + s + 1) * 2)
                        nc.scalar.activation(sg[s][:, 0:T], nat[s][:, :], ACT.Square).then_inc(sqr, 1)
                        act.wait_ge(eps, it * 2 + s + 1)
                        nc.scalar.activation(rn[s][:, :], rn[s][:, :], ACT.Sqrt).then_inc(root, 1)
                    if tok_out is not None:
                        act.wait_ge(tr, it * 2 + s + 1)
                        act.wait_ge(tst[s], (it + 1) * 16)
                        nc.scalar.activation(tok[s][:, :, :].rearrange("p t n -> p (t n)"),
                                             ps[s][:, :, :].rearrange("p b n -> p (b n)")[:, 0:T],
                                             ACT.Identity).then_inc(free, 1)

        @block.vector
        def _(dve):
            for s in range(2):
                nc.vector.memset(pad[s][:, :], 0.0).then_inc(zero, 1)
            dve.sem_inc(conv_d, 2 * TAPS)
            if tok_out is None:
                dve.sem_inc(free, 2)
            beside.chain_start(dve)
            with dve.Fori(0, U) as it:
                for s in range(2):
                    step = Steps(dve, conv_d, it * 2 + s + 2, TAPS)
                    dve.wait_ge(w_in[s], (it + 1) * 32)
                    dve.wait_ge(evac, (it * 2 + s + 1) * 2)
                    step(nc.vector.tensor_scalar(cv[s][:, :], pad[s][:, 0:WIDE], cw[s][:, 0:1], None, ALU.mult))
                    for j in range(1, TAPS):
                        step(nc.vector.scalar_tensor_tensor(out=cv[s][:, :], in0=pad[s][:, j:j + WIDE], scalar=cw[s][:, j:j + 1],
                                                            in1=cv[s][:, :], op0=ALU.mult, op1=ALU.add))
                    step.done()
                for s in range(2):
                    dve.wait_ge(sig, it * 2 + s + 1)
                    if chan_out is not None:
                        dve.wait_ge(cst[s], (it + 1) * 16)
                    for t0, at, n in ((0, 0, TC), (TC, XAT, TX)):
                        nc.vector.tensor_tensor(nat[s][:, t0:t0 + n], cv[s][:, at:at + n], sg[s][:, at:at + n],
                                                ALU.mult).then_inc(silu, 1)
                    if norm:
                        dve.wait_ge(ssum, it * 2 + s + 1)
                        nc.vector.tensor_scalar(rn[s][:, :], small[s][:, :], 1e-6, norm ** -2, ALU.add, ALU.mult).then_inc(eps, 1)
                        dve.wait_ge(root, it * 2 + s + 1)
                        nc.vector.reciprocal(rn[s][:, :], rn[s][:, :]).then_inc(inv, 1)
                        dve.wait_ge(bc, it * 2 + s + 1)
                        nc.vector.tensor_tensor(nat[s][:, :], nat[s][:, :], ps[s][:, :, :].rearrange("p b n -> p (b n)")[:, 0:T],
                                                ALU.mult).then_inc(nrm if tok_out is not None else free, 1)
                for s in range(2):
                    beside.chain(dve, it, s)

        @block.gpsimd
        def _(pool):
            beside.products(pool, 2 * U)


def silu_channels(nc, a, R, w, blocks, chan_out, beside=None):
    with Stage(nc) as st:
        w_sb = [st.sb("w_slot", [P, KC, P]) for _ in range(2)]
        sg = [st.sb("sigmoid", [P, T]) for _ in range(2)]
        z = [st.sb("silu", [P, T]) for _ in range(2)]
        ps = [st.ps("product_ps", [P, 3, 512]) for _ in range(2)]
        w_in = [st.sem("w_loaded") for _ in range(2)]
        mm = st.sem("product_ready")
        sig = st.sem("sigmoid_ready")
        silu = st.sem("silu_ready")
        stored = [st.sem("silu_stored") for _ in range(2)]
        if beside:
            beside.begin(st, blocks)
        block = st.block()
        U = blocks // 2

        @block.sync
        def _(sp):
            def load(it):
                for s in range(2):
                    sp.wait_ge(mm, it * 2 + s + 1)
                    sp.dma_start(w_sb[s][:, :, :], block_of(w, it * 2 + s)).then_inc(w_in[s], 16)
                    if beside:
                        beside.load(sp, it * 2 + s, s)

            def store(it):
                for s in range(2):
                    sp.wait_ge(silu, (it * 2 + s + 3) * 2)
                    sp.dma_start(chan_out[bass.ds((it * 2 + s) * P, P), :], z[s][:, :]).then_inc(stored[s], 16)

            for s in range(2):
                sp.sem_inc(stored[s], 16)
            load(0)
            with sp.Fori(0, U - 1) as it:
                load(it + 1)
                store(it)
            store(U - 1)
            for s in range(2):
                sp.wait_ge(stored[s], (U + 1) * 16)

        @block.tensor
        def _(pe):
            pe.sem_inc(mm, 2)
            with pe.Fori(0, U) as it:
                for s in range(2):
                    pe.wait_ge(w_in[s], (it + 1) * 16)
                    pe.wait_ge(silu, (it * 2 + s + 1) * 2)
                    product(nc, ps[s], w_sb[s], R["hT"]).then_inc(mm, 1)

        @block.scalar
        def _(act):
            with act.Fori(0, U) as it:
                for s in range(2):
                    act.wait_ge(mm, it * 2 + s + 3)
                    for part, t0, n in ((1, 0, TC), (0, TC, TX)):
                        nc.scalar.activation(sg[s][:, t0:t0 + n], in_psum(ps[s], part), ACT.Sigmoid).then_inc(sig, 1)

        @block.vector
        def _(dve):
            dve.sem_inc(silu, 4)
            if beside:
                beside.chain_start(dve)
            with dve.Fori(0, U) as it:
                for s in range(2):
                    dve.wait_ge(stored[s], (it + 1) * 16)
                    dve.wait_ge(sig, (it * 2 + s + 1) * 2)
                    for part, t0, n in ((1, 0, TC), (0, TC, TX)):
                        nc.vector.tensor_tensor(z[s][:, t0:t0 + n], sg[s][:, t0:t0 + n], in_psum(ps[s], part),
                                                ALU.mult).then_inc(silu, 1)
                    if beside:
                        beside.chain(dve, it, s)

        if beside:
            @block.gpsimd
            def _(pool):
                beside.products(pool, 2 * U)


KINDS = 7
CHUNK, SUB = 64, 16
H = 8


def gdn_gates(nc, a, R, w, a_log, dt_bias, gates):
    C = 32
    CT = TC // P
    NS, NCH = T // SUB, T // CHUNK
    PER = 2 * KINDS * H
    with Stage(nc) as st:
        w_sb = st.sb("w_slot", [P, KC, C])
        dtb = st.sb("dt_bias", [P, 2, H])
        shape = [P, NT + 1, 2, H]
        view = lambda t: t[:, :, :, :]
        F = Fused(nc, st, shape, view)
        v, u, ea, acc, *scratch = (st.sb(n, shape) for n in ("v", "u", "exp", "acc", *["scratch"] * 7))
        whole = st.sb("whole", shape, mybir.dt.int32)
        out = st.sb("gates", [P, NT, 2, KINDS, H])
        keep = st.sb("keep", [H, T])
        keep4 = st.sb("keep_sixteens", [H, NS])
        g = [st.sb("g_rows", [H, T]) for _ in range(2)]
        row = [st.sb("kind_rows", [H, KINDS - 1, T]) for _ in range(2)]
        tot, pre, sums = (st.sb(n, [H, NS]) for n in ("sixteens", "before", "up_to"))
        ps = st.ps("product_ps", [P, NT, 2, 2, H])
        turned = [st.ps("turned_ps", [P, 3, 512]) for _ in range(2)]
        loaded, mm, step_s = st.sem("loaded"), st.sem("product_ready"), st.sem("step_done")
        bet, stored = st.sem("beta_ready"), st.sem("gates_stored")
        g_ready, g_turned, rows_ready, back = st.sem("g_ready"), st.sem("g_turned"), st.sem("rows_ready"), st.sem("kinds_turned")
        ready = st.sem("gates_ready")
        block = st.block()

        @block.sync
        def _(sp):
            sp.dma_start(w_sb[:, :, :], w.rearrange("(k p) c -> p k c", p=P)).then_inc(loaded, 16)
            sp.dma_start(u[:, NT, :, :], a_log.rearrange("(o d) h -> o d h", o=1).to_broadcast([P, 2, H])).then_inc(loaded, 16)
            sp.dma_start(dtb[:, :, :], dt_bias.rearrange("(o d) h -> o d h", o=1).to_broadcast([P, 2, H])).then_inc(loaded, 16)
            sp.wait_ge(ready, 6)
            sp.wait_ge(bet, 1)
            sp.dma_start(gates.rearrange("(t p) c -> p t c", p=P), out[:, :, :, :, :].rearrange("p t d k h -> p t (d k h)")).then_inc(stored, 16)
            sp.wait_ge(stored, 16)

        @block.tensor
        def _(pe):
            pe.wait_ge(loaded, 48)
            for t in range(NT):
                for kc in range(KC):
                    last = nc.tensor.matmul(ps[:, t, :, :, :].rearrange("p d k h -> p (d k h)"), R["hT"][:, kc, t * P:(t + 1) * P],
                                            w_sb[:, kc, :], start=kc == 0, stop=kc == KC - 1)
            last.then_inc(mm, 1)
            pe.wait_ge(g_ready, 1)
            for d in range(2):
                for t in range(NT):
                    last = nc.tensor.transpose(turned[d][0:H, t // 4, t % 4 * P:t % 4 * P + P], acc[:, t, d, :], R["ident"][:, :])
                last.then_inc(g_turned, 1)
            for d in range(2):
                pe.wait_ge(rows_ready, d + 1)
                for t in range(NT):
                    for k in range(1, KINDS):
                        at = t % 4 * PER + (d * KINDS + k) * H
                        last = nc.tensor.transpose(turned[0][:, t // 4, at:at + H], row[d][:, k - 1, t * P:(t + 1) * P], R["ident"][0:H, 0:H])
                last.then_inc(back, 1)

        @block.scalar
        def _(act):
            act.wait_ge(mm, 1)
            nc.scalar.activation(out[:, :, :, 0, :], ps[:, :, :, 0, :], ACT.Sigmoid).then_inc(bet, 1)

        @block.vector
        def _(dve):
            V = nc.vector
            f = lambda x: x[:, :, :, :]
            step = Steps(dve, step_s)
            dve.wait_ge(bet, 1)
            dve.wait_ge(loaded, 48)
            bias = lambda n: dtb[:, :, :].rearrange("p (o d) h -> p o d h", o=1).to_broadcast([P, n, 2, H])
            chains = R["chains_ctx"][:, :, :].rearrange("p t (e d h) -> p t e d h", e=2, d=2)
            latent = slice(CT, NT)
            step(V.memset(f(v), 0.0))
            for t in range(CT):
                step(V.tensor_tensor(v[:, t], chains[:, t, 0], chains[:, t, 1], ALU.add))
            step(V.tensor_tensor(v[:, 0:CT], v[:, 0:CT], bias(CT), ALU.add))
            step(V.tensor_tensor(v[:, latent], ps[:, latent, :, 1, :], bias(NT - CT), ALU.add))
            step(V.scalar_tensor_tensor(out=u[:, 0:NT], in0=v[:, 0:NT], scalar=-1.0, in1=v[:, 0:NT], op0=ALU.mult, op1=ALU.min))
            F.exp(step, f(u), f(acc), f(ea), f(scratch[0]), f(whole))
            step(V.tensor_scalar(f(u), f(ea), 1.0, None, ALU.min))
            F.log1p(step, f(u), f(acc), [f(t) for t in scratch])
            step(V.scalar_tensor_tensor(out=f(acc), in0=f(v), scalar=0.0, in1=f(acc), op0=ALU.max, op1=ALU.add))
            scale = ea[:, NT:NT + 1].to_broadcast([P, NT, 2, H])
            V.scalar_tensor_tensor(out=acc[:, 0:NT], in0=acc[:, 0:NT], scalar=-1.0, in1=scale, op0=ALU.mult, op1=ALU.mult).then_inc(g_ready, 1)
            step(V.memset(keep[:, :], 1.0))
            step(V.memset(keep4[:, :], 1.0))
            step(V.memset(keep[:, :].rearrange("p (b n) -> p b n", n=SUB)[:, :, 0:1], 0.0))
            step(V.memset(keep4[:, :].rearrange("p (c b) -> p c b", b=CHUNK // SUB)[:, :, 0:1], 0.0))
            dve.wait_ge(g_turned, 2)
            for d in range(2):
                r = slice(None, None, -1) if d else slice(None)
                lastof = lambda n: n - 1 if d == 0 else 0
                B = CHUNK // SUB
                c, late, tile, total, to_end, first = (row[d][:, k, :] for k in range(KINDS - 1))
                chunked = lambda x: x.rearrange("p (t a n) -> p t a n", a=2, n=CHUNK)
                spread = lambda x: x.rearrange("p (t o) -> p t o", o=1).to_broadcast([H, NT, CHUNK])
                step(V.tensor_copy(g[d][:, :], turned[d][0:H, :, :].rearrange("p b n -> p (b n)")[:, 0:T]))
                step(V.tensor_tensor_scan(out=c[:, r], data0=keep[:, :], data1=g[d][:, r], initial=0.0, op0=ALU.mult, op1=ALU.add))
                step(V.tensor_copy(tot[:, :], c.rearrange("p (b n) -> p b n", n=SUB)[:, :, lastof(SUB)]))
                step(V.tensor_tensor_scan(out=sums[:, r], data0=keep4[:, :], data1=tot[:, r], initial=0.0, op0=ALU.mult, op1=ALU.add))
                by4 = lambda x: x[:, :].rearrange("p (c b) -> p c b", b=B)
                to, frm, none = (slice(1, B), slice(0, B - 1), slice(0, 1)) if d == 0 else (slice(0, B - 1), slice(1, B), slice(B - 1, B))
                step(V.tensor_copy(by4(pre)[:, :, to], by4(sums)[:, :, frm]))
                step(V.memset(by4(pre)[:, :, none], 0.0))
                step(V.tensor_tensor(c.rearrange("p (b n) -> p b n", n=SUB), c.rearrange("p (b n) -> p b n", n=SUB),
                                     pre[:, :].rearrange("p (b o) -> p b o", o=1).to_broadcast([H, NS, SUB]), ALU.add))
                ends = by4(sums)[:, :, lastof(B)].rearrange("p (t a) -> p t a", a=2)
                A, Z = d, 1 - d
                endA, endZ = (ends[:, :, i:i + 1].to_broadcast([H, NT, CHUNK]) for i in (A, Z))
                cA, cZ = chunked(c)[:, :, A, :], chunked(c)[:, :, Z, :]
                step(V.tensor_tensor(chunked(late)[:, :, A, :], cA, endA, ALU.subtract))
                step(V.tensor_copy(chunked(late)[:, :, Z, :], cZ))
                step(V.tensor_copy(chunked(tile)[:, :, A, :], cA))
                step(V.tensor_tensor(chunked(tile)[:, :, Z, :], cZ, endA, ALU.add))
                step(V.tensor_copy(chunked(first)[:, :, A, :], endA))
                step(V.tensor_copy(chunked(first)[:, :, Z, :], endA))
                for i in range(2):
                    step(V.tensor_tensor(chunked(total)[:, :, i, :], chunked(first)[:, :, i, :], endZ, ALU.add))
                step(V.tensor_tensor(chunked(to_end)[:, :, Z, :], endZ, cZ, ALU.subtract))
                V.tensor_tensor(chunked(to_end)[:, :, A, :], endZ, chunked(late)[:, :, A, :], ALU.subtract).then_inc(rows_ready, 1)
            dve.wait_ge(back, 2)
            for b in range(3):
                n = min(4, NT - 4 * b)
                view = turned[0][:, b, 0:n * PER].rearrange("p (t d c) -> p t d c", t=n, d=2)
                for d in range(2):
                    V.tensor_copy(out[:, 4 * b:4 * b + n, d, 1:KINDS, :].rearrange("p t k h -> p t (k h)"), view[:, :, d, H:]).then_inc(ready, 1)




class Inverse:

    def __init__(self, nc, st, masks):
        self.nc, self.masks = nc, masks
        self.kept_pair = [st.sb("inverse", [P, 2, 2, P]) for _ in range(2)]
        self.tick = [st.sb("tick", [1, 1]) for _ in range(2)]
        self.joins = {}
        self.p_ps = [st.ps("at_ps", [P, 2, P]) for _ in range(2)]
        self.t_ps = [st.ps("inverse_ps", [P, 2, 2, P]) for _ in range(2)]
        self.at_ready, self.join_ready = st.sem("at_ready"), st.sem("join_ready")
        self.new_ready, self.kept = st.sem("new_inverse_ready"), st.sem("inverse_kept")
        self.joins_set = st.sem("joins_set")

    def transposed(self, h):
        return self.kept_pair[h // 2][:, 1, h % 2, :]

    def wait_kept(self, eng, u):
        eng.wait_ge(self.kept, (u + 1) * (2 * LEVELS))

    def tensor(self, pe, u, na, ident, beside={}):
        for k in range(LEVELS):
            join = self.joins[self.dir, k]
            count = lambda level, pair: u * (2 * LEVELS) + (level * 2 + pair + 1)
            for pair in range(2):
                if k > 0:
                    pe.wait_ge(self.kept, count(k - 1, pair))
                for h in range(2):
                    last = self.nc.tensor.matmul(self.p_ps[pair][:, h, :], na[:, 2 * pair + h, :],
                                                 ident[:, :] if k == 0 else self.kept_pair[pair][:, 0, h, :], start=True, stop=True)
                last.then_inc(self.at_ready, 1)
            for pair in range(2):
                pe.wait_ge(self.join_ready, count(k, pair))
                for h in range(2):
                    j = join[:, 2 * pair + h, :]
                    tt = ident[:, :] if k == 0 else self.kept_pair[pair][:, 1, h, :]
                    if k < LEVELS - 1:
                        self.nc.tensor.matmul(self.t_ps[pair][:, 0, h, :], tt, j, start=True, stop=True)
                    last = self.nc.tensor.matmul(self.t_ps[pair][:, 1, h, :], j, tt, start=True, stop=True)
                last.then_inc(self.new_ready, 1)
            if k in beside:
                beside[k]()

    def vector(self, dve, u, beside={}):
        for k in range(LEVELS):
            mask = self.masks[:, self.dir * LEVELS + k:self.dir * LEVELS + k + 1, :].to_broadcast([P, 2, P])
            for pair in range(2):
                dve.wait_ge(self.at_ready, u * (2 * LEVELS) + (2 * k + pair + 1))
                self.nc.vector.memset(self.tick[pair][:, :], 0.0)
                self.nc.vector.copy_predicated(self.joins[self.dir, k][:, 2 * pair:2 * pair + 2, :], mask,
                                               self.p_ps[pair][:, :, :]).then_inc(self.join_ready, 1)
            if k in beside:
                beside[k]()

    def scalar(self, act, u, beside={}):
        for k in range(LEVELS):
            kinds = slice(0, 2) if k < LEVELS - 1 else slice(1, 2)
            for pair in range(2):
                act.wait_ge(self.new_ready, u * (2 * LEVELS) + (2 * k + pair + 1))
                self.nc.scalar.copy(self.kept_pair[pair][:, kinds, :, :], self.t_ps[pair][:, kinds, :, :]).then_inc(self.kept, 1)
            if k in beside:
                beside[k]()


def head_bcast(ap, n=P):
    return ap.rearrange("p (h o) -> p h o", o=1).to_broadcast([P, ap.shape[-1], n])


def tile_at(d, it):
    return it if d == 0 else (it * (NT - 1) + 1) % NT


def chunk_cols(d):
    return (slice(0, P // 2), slice(P // 2, P))[::1 if d == 0 else -1]


def gdn_scan(nc, R, S, chan_out):
    G = 4
    with Stage(nc) as st:
        kq = [st.sb("k_q_by_channel", [P, 4, 2, P]) for _ in range(2)]
        kt = [st.sb("k_by_token", [P, 4, P]) for _ in range(2)]
        vt = [st.sb("v_by_token", [P, 4, P]) for _ in range(2)]
        gb = [st.sb("gates", [P, KINDS, 4]) for _ in range(2)]
        state = [st.sb("state", [P, 4, P]) for _ in range(G)]
        exps = st.sb("exp_sums", [P, 12])
        nbe = st.sb("minus_beta_decay", [P, 4])
        dif, dec, bdec, na, qk = (st.sb(n, [P, 4, P]) for n in ("differences", "decays", "beta_decays", "minus_a", "qk"))
        egr, qg, bv, rhs, upd, kd, o_sb = (st.sb(n, [P, 4, P]) for n in (
            "row_decay", "q_decayed", "beta_v", "rhs", "updates", "k_to_end", "o_out"))
        inv = Inverse(nc, st, R["join_masks"])
        for d in range(2):
            for k in range(LEVELS):
                inv.joins[d, k] = st.sb("join", [P, 4, P])
        row_ps = st.ps("rows_ps", [P, 4, P])
        beta_ps = st.ps("beta_ps", [P, 4, P])
        kkq_ps = st.ps("kk_kq_ps", [P, 4, 2, P])
        flat = kkq_ps[:, :, :, :].rearrange("p h n t -> p (h n) t")
        o_ps, ds_ps = flat[:, 0:4, :], flat[:, 4:8, :]
        loaded = [st.sem("group_loaded") for _ in range(2)]
        zeroed, rows_s, kkq_s, ks_s, o_s = (st.sem(n) for n in (
            "state_zeroed", "rows_ready", "products_ready", "ks_ready", "output_ready"))
        upd_s = st.sem("updates_ready")
        used = st.sem("group_used")
        o_kept = st.sem("output_kept")
        o_stored = st.sem("output_stored")
        v_step = st.sem("vector_step")
        a_step, p_step = st.sem("scalar_step"), st.sem("pool_step")
        block = st.block()
        VS, AS, PS = 12, 5, 3

        @block.sync
        def _(sp):
            def load(it, g):
                d, half, s = g // 2, g % 2, g % 2
                t = tile_at(d, it)
                cols = slice(half * 512, half * 512 + 512)
                sp.wait_ge(used, it * G + g + 1)
                for n, src in ((0, "kT"), (1, "qT")):
                    sp.dma_start(kq[s][:, :, n, :], S[src][cols, bass.ds(t * P, P)].rearrange("(h p) t -> p h t", p=P)
                                 ).then_inc(loaded[s], 16)
                for dst, src in ((kt, "ktok"), (vt, "vtok")):
                    sp.dma_start(dst[s][:, :, :].rearrange("p h n -> p (h n)"), S[src][bass.ds(t * P, P), cols]).then_inc(loaded[s], 16)
                gates = S["gates"].rearrange("t (d k h) -> t d k h", d=2, k=KINDS)
                with nc.allow_non_contiguous_dma("4 values a kind"):
                    sp.dma_start(gb[s][:, :, :], gates[bass.ds(t * P, P), d, :, half * 4:half * 4 + 4]).then_inc(loaded[s], 16)

            def store(it, g):
                d, half = g // 2, g % 2
                t = tile_at(d, it)
                sp.wait_ge(o_kept, it * G + g + 2)
                sp.dma_start(chan_out[d][half * 512:half * 512 + 512, bass.ds(t * P, P)].rearrange("(h p) t -> p h t", p=P),
                             o_sb[:, :, :]).then_inc(o_stored, 16)

            sp.sem_inc(o_stored, 16)
            with sp.Fori(0, NT) as it:
                load(it, 0)
                for g in range(1, G):
                    load(it, g)
                    store(it, g - 1)
                store(it, G - 1)
            sp.wait_ge(o_stored, (NT * G + 1) * 16)

        @block.gpsimd
        def _(pool):
            for g in range(G):
                nc.gpsimd.memset(state[g][:, :, :], 0.0).then_inc(zeroed, 1)
            with pool.Fori(0, NT) as it:
                for g in range(G):
                    u, s = it * G + g, g % 2
                    step = Steps(pool, p_step, u, PS)
                    pool.wait_ge(loaded[s], (it * 2 + g // 2 + 1) * 80)
                    pool.wait_ge(upd_s, u + 1)
                    step(nc.gpsimd.tensor_tensor(bv[:, :, :], vt[s][:, :, :], head_bcast(gb[s][:, 0, :]), ALU.mult))
                    pool.wait_ge(a_step, u * AS + 4)
                    step(nc.gpsimd.tensor_tensor(qg[:, :, :], kq[s][:, :, 1, :], egr[:, :, :], ALU.mult))
                    step(nc.gpsimd.tensor_tensor(kd[:, :, :], kt[s][:, :, :], head_bcast(exps[:, 8:12]), ALU.mult))
                    step.done()

        @block.tensor
        def _(pe):
            pe.sem_inc(upd_s, 1)
            pe.sem_inc(used, 2)
            pe.wait_ge(inv.joins_set, 2 * LEVELS)
            pe.wait_ge(zeroed, G)
            with pe.Fori(0, NT) as it:
                for g in range(G):
                    u, s, d = it * G + g, g % 2, g // 2
                    inv.dir = d
                    c, beta = gb[s][:, 1, :], gb[s][:, 0, :]
                    pe.wait_ge(loaded[s], (it * 2 + g // 2 + 1) * 80)
                    pe.wait_ge(v_step, (u + 1) * VS)
                    pe.wait_ge(o_kept, u + 1)
                    for h in range(4):
                        nc.tensor.matmul(row_ps[:, h, :], c[:, h:h + 1].to_broadcast([P, P]), R["ident"][:, :],
                                         start=True, stop=True)
                    for h in range(4):
                        last = nc.tensor.matmul(beta_ps[:, h, :], beta[:, h:h + 1].to_broadcast([P, P]), R["ident"][:, :],
                                                start=True, stop=True)
                    last.then_inc(rows_s, 1)
                    for h in range(4):
                        last = nc.tensor.matmul(kkq_ps[:, h, :, :].rearrange("p n t -> p (n t)"), kq[s][:, h, 0, :],
                                                kq[s][:, h, :, :].rearrange("p n t -> p (n t)"), start=True, stop=True)
                    last.then_inc(kkq_s, 1)

                    def keys_with_state():
                        pe.wait_ge(a_step, u * AS + 4)
                        for h in range(4):
                            last = nc.tensor.matmul(row_ps[:, h, :], kq[s][:, h, 0, :], state[g][:, h, :], start=True, stop=True)
                        last.then_inc(ks_s, 1)

                    pe.wait_ge(v_step, u * VS + VS + 6)
                    inv.tensor(pe, u, na, R["ident"], {1: keys_with_state})
                    pe.wait_ge(v_step, u * VS + VS + 10)
                    inv.wait_kept(pe, u)
                    for h in range(4):
                        last = nc.tensor.matmul(beta_ps[:, h, :], inv.transposed(h), rhs[:, h, :], start=True, stop=True)
                    last.then_inc(upd_s, 1)
                    pe.wait_ge(a_step, u * AS + 5)
                    pe.wait_ge(p_step, u * PS + PS)
                    for h in range(4):
                        nc.tensor.matmul(o_ps[:, h, :], state[g][:, h, :], qg[:, h, :], start=True, stop=False)
                        last = nc.tensor.matmul(o_ps[:, h, :], upd[:, h, :], qk[:, h, :], start=False, stop=True)
                    last.then_inc(o_s, 1)
                    for h in range(4):
                        last = nc.tensor.matmul(ds_ps[:, h, :], kd[:, h, :], upd[:, h, :], start=True, stop=True)
                    last.then_inc(used, 1)

        @block.scalar
        def _(act):
            act.sem_inc(o_kept, 1)
            with act.Fori(0, NT) as it:
                for g in range(G):
                    u, s, d = it * G + g, g % 2, g // 2
                    inv.dir = d
                    A, Z = chunk_cols(d)
                    step = Steps(act, a_step, u, AS)
                    act.wait_ge(loaded[s], (it * 2 + g // 2 + 1) * 80)
                    act.wait_ge(v_step, (u + 1) * VS)
                    step(nc.scalar.activation(exps[:, :], gb[s][:, 3:6, :].rearrange("p k h -> p (k h)"), ACT.Exp))
                    act.wait_ge(v_step, u * VS + VS + 4)
                    step(nc.scalar.activation(dec[:, :, :], dif[:, :, :], ACT.Exp))

                    def row_decays():
                        step(nc.scalar.activation(egr[:, :, A], row_ps[:, :, A], ACT.Exp))
                        step(nc.scalar.activation(egr[:, :, Z], egr[:, :, Z], ACT.Exp))

                    inv.scalar(act, u, {0: row_decays})
                    act.wait_ge(upd_s, u + 2)
                    step(nc.scalar.copy(upd[:, :, :], beta_ps[:, :, :]))
                    step.done()
                    act.wait_ge(o_s, u + 1)
                    act.wait_ge(o_stored, (u + 1) * 16)
                    nc.scalar.copy(o_sb[:, :, :], o_ps).then_inc(o_kept, 1)

        @block.vector
        def _(dve):
            dve.sem_inc(v_step, VS)
            for join in inv.joins.values():
                nc.vector.tensor_copy(join[:, :, :], R["ident"][:, :].rearrange("p (o n) -> p o n", o=1).to_broadcast([P, 4, P])
                                      ).then_inc(inv.joins_set, 1)
            dve.wait_ge(inv.joins_set, 2 * LEVELS)
            dve.wait_ge(zeroed, G)
            with dve.Fori(0, NT) as it:
                for g in range(G):
                    u, s, d = it * G + g, g % 2, g // 2
                    inv.dir = d
                    step = Steps(dve, v_step, u + 1, VS)
                    A, Z = chunk_cols(d)
                    dve.wait_ge(rows_s, u + 1)
                    step(nc.vector.tensor_tensor(dif[:, :, A], row_ps[:, :, A], head_bcast(gb[s][:, 1, :], P // 2), ALU.subtract))
                    step(nc.vector.tensor_tensor(dif[:, :, Z], row_ps[:, :, Z], head_bcast(gb[s][:, 2, :], P // 2), ALU.subtract))
                    step(nc.vector.tensor_tensor(egr[:, :, Z], row_ps[:, :, Z], head_bcast(gb[s][:, 6, :], P // 2), ALU.add))
                    off = R["off"][:, d:d + 1, :].to_broadcast([P, 4, P])
                    step(nc.vector.scalar_tensor_tensor(out=dif[:, :, :], in0=dif[:, :, :], scalar=0.0, in1=off,
                                                        op0=ALU.min, op1=ALU.add))
                    dve.wait_ge(a_step, u * AS + 2)
                    step(nc.vector.tensor_tensor(bdec[:, :, :], dec[:, :, :], beta_ps[:, :, :], ALU.mult))
                    dve.wait_ge(kkq_s, u + 1)
                    step(nc.vector.scalar_tensor_tensor(out=na[:, :, :], in0=kkq_ps[:, :, 0, :], scalar=-1.0, in1=bdec[:, :, :],
                                                        op0=ALU.mult, op1=ALU.mult))

                    def decayed_products():
                        step(nc.vector.tensor_tensor(qk[:, :, :], kkq_ps[:, :, 1, :], dec[:, :, :], ALU.mult))
                        step(nc.vector.scalar_tensor_tensor(out=nbe[:, :], in0=exps[:, 0:4], scalar=-1.0, in1=gb[s][:, 0, :],
                                                            op0=ALU.mult, op1=ALU.mult))

                    def right_side():
                        dve.wait_ge(ks_s, u + 1)
                        step(nc.vector.tensor_tensor(rhs[:, :, :], row_ps[:, :, :], head_bcast(nbe[:, :]), ALU.mult))
                        dve.wait_ge(p_step, u * PS + 1)
                        step(nc.vector.tensor_tensor(rhs[:, :, :], rhs[:, :, :], bv[:, :, :], ALU.add))

                    inv.vector(dve, u, {0: decayed_products, 3: right_side})
                    dve.wait_ge(o_s, u + 1)
                    step(nc.vector.tensor_tensor(state[g][:, :, :], state[g][:, :, :], head_bcast(exps[:, 4:8]), ALU.mult))
                    dve.wait_ge(used, u + 3)
                    step(nc.vector.tensor_tensor(state[g][:, :, :], state[g][:, :, :], ds_ps, ALU.add))
                    step.done()


def plain_channels(nc, R, w, blocks, chan_out=None, tok_out=None):
    with Stage(nc) as st:
        w_sb = [st.sb("w_slot", [P, KC, P]) for _ in range(2)]
        y = [st.sb("by_channel", [P, T]) for _ in range(2)]
        tok = [st.sb("by_token", [P, NT, P]) for _ in range(2)] if tok_out is not None else None
        ps = [st.ps("product_ps", [P, 3, 512]) for _ in range(2)]
        w_in = [st.sem("w_loaded") for _ in range(2)]
        mm = st.sem("product_ready")
        kept = st.sem("product_kept")
        turned = st.sem("turned_ready")
        tok_kept = st.sem("turned_kept")
        cst = [st.sem("channels_stored") for _ in range(2)]
        tst = [st.sem("tokens_stored") for _ in range(2)]
        block = st.block()
        U = blocks // 2

        @block.sync
        def _(sp):
            def load(it):
                for s in range(2):
                    sp.wait_ge(mm, it * 2 + s + 1)
                    sp.dma_start(w_sb[s][:, :, :], block_of(w, it * 2 + s)).then_inc(w_in[s], 16)

            def store(it):
                for s in range(2):
                    if chan_out is not None:
                        sp.wait_ge(kept, (it * 2 + s + 3) * 2)
                        sp.dma_start(chan_out[bass.ds((it * 2 + s) * P, P), :], y[s][:, :]).then_inc(cst[s], 16)
                    if tok_out is not None:
                        sp.wait_ge(tok_kept, it * 2 + s + 3)
                        sp.dma_start(tok_out.rearrange("(t p) c -> p t c", p=P)[:, :, bass.ds(it * (2 * P) + s * P, P)],
                                     tok[s][:, :, :]).then_inc(tst[s], 16)

            for s in range(2):
                sp.sem_inc(cst[s], 16)
                sp.sem_inc(tst[s], 16)
            load(0)
            with sp.Fori(0, U - 1) as it:
                load(it + 1)
                store(it)
            store(U - 1)
            for s in range(2):
                if chan_out is not None:
                    sp.wait_ge(cst[s], (U + 1) * 16)
                if tok_out is not None:
                    sp.wait_ge(tst[s], (U + 1) * 16)

        @block.tensor
        def _(pe):
            pe.sem_inc(mm, 2)
            with pe.Fori(0, U) as it:
                for s in range(2):
                    pe.wait_ge(w_in[s], (it + 1) * 16)
                    pe.wait_ge(kept, (it * 2 + s + 1) * 2)
                    if tok_out is not None:
                        pe.wait_ge(tok_kept, it * 2 + s + 1)
                    product(nc, ps[s], w_sb[s], R["hT"]).then_inc(mm, 1)
                if tok_out is not None:
                    for s in range(2):
                        pe.wait_ge(kept, (it * 2 + s + 3) * 2)
                        flat = ps[s][:, :, :].rearrange("p b n -> p (b n)")
                        for t in range(NT):
                            last = nc.tensor.transpose(flat[:, t * P:(t + 1) * P], y[s][:, t * P:(t + 1) * P], R["ident"][:, :])
                        last.then_inc(turned, 1)

        @block.scalar
        def _(act):
            act.sem_inc(kept, 4)
            with act.Fori(0, U) as it:
                for s in range(2):
                    if chan_out is not None:
                        act.wait_ge(cst[s], (it + 1) * 16)
                    act.wait_ge(mm, it * 2 + s + 3)
                    for part, t0, n in ((1, 0, TC), (0, TC, TX)):
                        nc.scalar.copy(y[s][:, t0:t0 + n], in_psum(ps[s], part)).then_inc(kept, 1)

        if tok_out is not None:
            @block.vector
            def _(dve):
                dve.sem_inc(tok_kept, 2)
                with dve.Fori(0, U) as it:
                    for s in range(2):
                        dve.wait_ge(tst[s], (it + 1) * 16)
                        dve.wait_ge(turned, it * 2 + s + 1)
                        nc.vector.tensor_copy(tok[s][:, :, :].rearrange("p t n -> p (t n)"),
                                              ps[s][:, :, :].rearrange("p b n -> p (b n)")[:, 0:T]).then_inc(tok_kept, 1)


def shift_tokens(nc, R, xx):
    with Stage(nc) as st:
        step_s = st.sem("shift_step")
        block = st.block()

        @block.vector
        def _(dve):
            n = 0
            for t0, L in ((0, TC), (TC, TX)):
                h, o = R["hT"][:, :, t0:t0 + L], xx[:, :, t0:t0 + L]
                for kc in range(KC):
                    nc.vector.tensor_tensor(o[:, kc, 1:L - 1], h[:, kc, 0:L - 2], h[:, kc, 2:L], ALU.add).then_inc(step_s, 1)
                nc.vector.tensor_copy(o[:, :, 0:1], h[:, :, 1:2]).then_inc(step_s, 1)
                nc.vector.tensor_copy(o[:, :, L - 1:L], h[:, :, L - 2:L - 1]).then_inc(step_s, 1)
                n += KC + 2
            dve.wait_ge(step_s, n)
            for kc in range(KC):
                nc.vector.scalar_tensor_tensor(out=xx[:, kc, :], in0=xx[:, kc, :], scalar=0.5, in1=R["hT"][:, kc, :],
                                               op0=ALU.mult, op1=ALU.subtract).then_inc(step_s, 1)
            dve.wait_ge(step_s, n + KC)


def mix_tokens(nc, R, xx, mu, mx):
    with Stage(nc) as st:
        m = st.sb("mu", [P, KC])
        loaded, mixed = st.sem("mu_loaded"), st.sem("mixed")
        block = st.block()

        @block.sync
        def _(sp):
            with nc.allow_non_contiguous_dma("8 values a partition"):
                sp.dma_start(m[:, :], mu.rearrange("(k p) -> p k", p=P)).then_inc(loaded, 16)

        @block.vector
        def _(dve):
            dve.wait_ge(loaded, 16)
            for kc in range(KC):
                nc.vector.scalar_tensor_tensor(out=mx[:, kc, :], in0=xx[:, kc, :], scalar=m[:, kc:kc + 1],
                                               in1=R["hT"][:, kc, :], op0=ALU.mult, op1=ALU.add).then_inc(mixed, 1)


def low_rank(nc, R, w_cols, out, tanh):
    with Stage(nc) as st:
        M = out.shape[0]
        w_sb = st.sb("w_slot", [P, KC, M])
        ps = st.ps("product_ps", [P, 3, 512])
        loaded, mm, kept = st.sem("w_loaded"), st.sem("product_ready"), st.sem("kept")
        block = st.block()

        @block.sync
        def _(sp):
            for c0, w in w_cols:
                sp.dma_start(w_sb[:, :, c0:c0 + w.shape[1]], w.rearrange("(k p) c -> p k c", p=P)).then_inc(loaded, 16)

        @block.tensor
        def _(pe):
            pe.wait_ge(loaded, 16 * len(w_cols))
            product(nc, ps[0:M], w_sb, R["hT"]).then_inc(mm, 1)

        @block.scalar
        def _(act):
            act.wait_ge(mm, 1)
            for part, t0, n in ((1, 0, TC), (0, TC, TX)):
                nc.scalar.activation(out[:, t0:t0 + n], in_psum(ps[0:M], part), ACT.Tanh if tanh else ACT.Identity).then_inc(kept, 1)


class Track:

    def __init__(self, sem, names, lead=0):
        self.sem, self.names, self.lead, self.n = sem, names.split(), lead, 0

    def start(self, eng):
        if self.lead:
            eng.sem_inc(self.sem, self.lead * len(self.names))

    def done(self, ins, name):
        assert self.names[self.n % len(self.names)] == name, (name, self.names[self.n % len(self.names)])
        self.n += 1
        ins.then_inc(self.sem, 1)

    def wait(self, eng, it, name):
        eng.wait_ge(self.sem, (it + self.lead) * len(self.names) + (self.names.index(name) + 1))

    def wait_last(self, eng, it):
        eng.wait_ge(self.sem, (it + self.lead) * len(self.names))


NATURAL = ((0, 512), (512, 512), (1024, 256))


def direction(d):
    return slice(None, None, -1) if d else slice(None)


def rwkv_prepare(nc, a, R, S, lw, la, rT, kT, vT, bonusT):
    with Stage(nc) as st:
        r, k, v, kk, bon, kx, e1, e2, e3, c, cx, kd, t1 = (st.sb(n, [P, T]) for n in (
            "r", "k", "v", "kk", "bonus", "k_scaled", "exp_c", "exp_minus_c", "exp_c_before", "c", "c_before", "k_dir", "t1"))
        av, lg = st.sb("rate", [P, T]), st.sb("log_decay", [P, T])
        o = [[R["hT"][:, 4 * d + i, :] for i in range(4)] for d in range(2)]
        tok = [st.sb("by_token", [P, NT, P]) for _ in range(2)]
        edge = [st.sb("edges", [P, 2, NT]) for _ in range(2)]
        ends = st.sb("edge_logs", [P, 2, NT])
        keep = st.sb("keep", [P, T])
        keep_s = st.sem("keep_set")
        prm = st.sb("channel_values", [P, 7])
        w2 = st.sb("w2_slot", [P, 2, P])
        ps = [st.ps("ps", [P, 3, 512]) for _ in range(2)]
        flat = [p[:, :, :].rearrange("p b n -> p (b n)")[:, 0:T] for p in ps]
        loaded = st.sem("block_loaded")
        stored = [st.sem("direction_stored") for _ in range(2)]
        bonus_stored = st.sem("bonus_stored")
        STORES = 7 * 16
        pe_t = Track(st.sem("tensor_did"), "len w0 a0 bon0 tk0 tq0 w1 a1 bon1 tk1 tq1")
        act_t = Track(st.sem("scalar_did"), "sq root wsig0 asig0 edge0 e10 e20 e30 tok00 tok01 wsig1 asig1 edge1 e11 e21 e31 tok10 tok11")
        per_d = "lg{0} scan{0} mid{0} end{0} cref{0} cx{0} am{0} kd{0} rp{0} kkp{0} ka{0} kkap{0} kp{0} bsrc{0}"
        dve_t = Track(st.sem("vector_did"), "kx eps rinv kk " + per_d.format(0) + " " + per_d.format(1) + " bonus", lead=1)
        block = st.block()

        @block.sync
        def _(sp):
            sp.sem_inc(bonus_stored, 16)
            for d in range(2):
                sp.sem_inc(stored[d], STORES)
            with sp.Fori(0, KC) as b:
                rows = bass.ds(b * P, P)
                dve_t.wait_last(sp, b)
                for dst, src in ((r, rT), (k, kT), (v, vT)):
                    sp.dma_start(dst[:, :], src[rows, :]).then_inc(loaded, 16)
                with nc.allow_non_contiguous_dma("one value a partition"):
                    for i, src in enumerate((a["rwkv_w0"][0, 0], a["rwkv_w0"][0, 1], a["rwkv_a0"][0, 0], a["rwkv_a0"][0, 1],
                                             a["rwkv_k_k"][0], a["rwkv_k_a"][0], a["rwkv_r_k"][0].rearrange("h d -> (h d)"))):
                        sp.dma_start(prm[:, i:i + 1], src[rows].rearrange("(p o) -> p o", o=1)).then_inc(loaded, 16)
                for i, src in enumerate((a["rwkv_w2"], a["rwkv_a2"])):
                    sp.dma_start(w2[:, i, :], src[0].rearrange("n r c -> (n r) c")[:, rows]).then_inc(loaded, 16)
                for d in range(2):
                    dve_t.wait(sp, b, f"kp{d}")
                    for i, name in enumerate(("kkp", "rp", "kkap", "kp")):
                        sp.dma_start(S[name][d][rows, :], o[d][i][:, :]).then_inc(stored[d], 16)
                    act_t.wait(sp, b, f"tok{d}1")
                    sp.dma_start(S["edges"][d][rows, :, :], edge[d][:, :, :]).then_inc(stored[d], 16)
                    for i, name in enumerate(("kkatok", "ktok2")):
                        sp.dma_start(S[name][d].rearrange("(t p) c -> p t c", p=P)[:, :, rows], tok[i][:, :, :]).then_inc(stored[d], 16)
                dve_t.wait(sp, b, "bonus")
                sp.dma_start(bonusT[rows, :], bon[:, :]).then_inc(bonus_stored, 16)
            for d in range(2):
                sp.wait_ge(stored[d], (KC + 1) * STORES)
            sp.wait_ge(bonus_stored, (KC + 1) * 16)

        @block.tensor
        def _(pe):
            def spread(out, weights, moving, start=True, stop=True):
                for bank, (t0, n) in enumerate(NATURAL):
                    last = nc.tensor.matmul(out[:, bank, 0:n], weights, moving[:, t0:t0 + n], start=start, stop=stop)
                return last

            with pe.Fori(0, KC) as b:
                pe.wait_ge(loaded, (b + 1) * 12 * 16)
                act_t.wait(pe, b, "sq")
                pe_t.done(spread(ps[0], R["head_ones"][:, :], e1), "len")
                for d in range(2):
                    rk = slice(d * 64, d * 64 + 64)
                    if d == 1:
                        act_t.wait(pe, b, "tok01")
                    pe_t.done(spread(ps[1], w2[rk, 0, :], lw[rk, :]), f"w{d}")
                    act_t.wait(pe, b, f"wsig{d}")
                    pe_t.done(spread(ps[1], w2[rk, 1, :], la[rk, :]), f"a{d}")
                    dve_t.wait(pe, b, f"bsrc{d}")
                    pe_t.done(spread(ps[0], R["head_ones"][:, :], t1, start=d == 0, stop=d == 1), f"bon{d}")
                    act_t.wait(pe, b, f"asig{d}")
                    for i, name in enumerate(("tk", "tq")):
                        if i == 1:
                            act_t.wait(pe, b, f"tok{d}0")
                        for t in range(NT):
                            last = nc.tensor.transpose(flat[1][:, t * P:(t + 1) * P], o[d][2 + i][:, t * P:(t + 1) * P],
                                                       R["ident"][:, :])
                        pe_t.done(last, f"{name}{d}")

        @block.scalar
        def _(act):
            A = nc.scalar.activation
            with act.Fori(0, KC) as b:
                dve_t.wait(act, b, "kx")
                act_t.done(A(e1[:, :], kx[:, :], ACT.Square), "sq")
                dve_t.wait(act, b, "eps")
                act_t.done(A(e2[:, :], e2[:, :], ACT.Sqrt), "root")
                for d in range(2):
                    dve_t.wait(act, b, "kk" if d == 0 else "kp0")
                    if d == 1:
                        dve_t.wait(act, b, "bsrc0")
                    pe_t.wait(act, b, f"w{d}")
                    act_t.done(A(lg[:, :], flat[1], ACT.Sigmoid, bias=prm[:, d:d + 1]), f"wsig{d}")
                    pe_t.wait(act, b, f"a{d}")
                    act_t.done(A(av[:, :], flat[1], ACT.Sigmoid, bias=prm[:, 2 + d:3 + d]), f"asig{d}")
                    act.wait_ge(stored[d], (b + 1) * STORES)
                    dve_t.wait(act, b, f"cx{d}")
                    act_t.done(A(edge[d][:, :, :], ends[:, :, :], ACT.Exp), f"edge{d}")
                    act_t.done(A(e1[:, :], c[:, :], ACT.Exp), f"e1{d}")
                    act_t.done(A(e2[:, :], c[:, :], ACT.Exp, scale=-1.0), f"e2{d}")
                    act_t.done(A(e3[:, :], cx[:, :], ACT.Exp), f"e3{d}")
                    if d == 1:
                        act.wait_ge(stored[0], (b + 2) * STORES)
                    else:
                        act.wait_ge(stored[1], (b + 1) * STORES)
                    for i, name in enumerate(("tk", "tq")):
                        pe_t.wait(act, b, f"{name}{d}")
                        act_t.done(nc.scalar.copy(tok[i][:, :, :].rearrange("p t n -> p (t n)"), flat[1]), f"tok{d}{i}")

        @block.vector
        def _(dve):
            V = nc.vector
            dve_t.start(dve)
            V.memset(keep[:, :], 1.0).then_inc(keep_s, 1)
            dve.wait_ge(keep_s, 1)
            V.memset(keep[:, :].rearrange("p (t n) -> p t n", n=P)[:, :, 0:1], 0.0).then_inc(keep_s, 1)
            dve.wait_ge(keep_s, 2)
            with dve.Fori(0, KC) as b:
                def did(ins, name):
                    dve_t.done(ins, name)
                    dve_t.wait(dve, b, name)

                dve.wait_ge(loaded, (b + 1) * 12 * 16)
                did(V.tensor_scalar(kx[:, :], k[:, :], prm[:, 4:5], None, ALU.mult), "kx")
                pe_t.wait(dve, b, "len")
                did(V.tensor_scalar(e2[:, :], flat[0], 1e-6, None, ALU.add), "eps")
                act_t.wait(dve, b, "root")
                did(V.reciprocal(e2[:, :], e2[:, :]), "rinv")
                did(V.tensor_tensor(kk[:, :], kx[:, :], e2[:, :], ALU.mult), "kk")
                for d in range(2):
                    f = direction(d)
                    by_tile = lambda x: x[:, :].rearrange("p (t n) -> p t n", n=P)
                    mid, end = (P // 2, P - 1) if d == 0 else (P // 2 - 1, 0)
                    act_t.wait(dve, b, f"asig{d}")
                    did(V.tensor_scalar(lg[:, :], lg[:, :], -math.exp(-0.5), None, ALU.mult), f"lg{d}")
                    did(V.tensor_tensor_scan(out=c[:, f], data0=keep[:, :], data1=lg[:, f], initial=0.0,
                                             op0=ALU.mult, op1=ALU.add), f"scan{d}")
                    did(V.tensor_copy(ends[:, 0, :], by_tile(c)[:, :, mid]), f"mid{d}")
                    did(V.tensor_tensor(ends[:, 1, :], by_tile(c)[:, :, end], ends[:, 0, :], ALU.subtract), f"end{d}")
                    did(V.tensor_tensor(by_tile(c), by_tile(c), ends[:, 0, :].rearrange("p (t o) -> p t o", o=1).to_broadcast([P, NT, P]),
                                        ALU.subtract), f"cref{d}")
                    did(V.tensor_tensor(cx[:, :], c[:, :], lg[:, :], ALU.subtract), f"cx{d}")
                    did(V.tensor_scalar(kd[:, :], av[:, :], 1.0, prm[:, 5:6], ALU.subtract, ALU.mult), f"am{d}")
                    did(V.scalar_tensor_tensor(out=kd[:, :], in0=kd[:, :], scalar=1.0, in1=k[:, :], op0=ALU.add, op1=ALU.mult), f"kd{d}")
                    act_t.wait(dve, b, f"e3{d}")
                    dve.wait_ge(stored[d], (b + 1) * STORES)
                    did(V.tensor_tensor(o[d][1][:, :], r[:, :], e1[:, :], ALU.mult), f"rp{d}")
                    did(V.tensor_tensor(o[d][0][:, :], kk[:, :], e3[:, :], ALU.mult), f"kkp{d}")
                    if d == 1:
                        pe_t.wait(dve, b, "bon0")
                    did(V.tensor_tensor(t1[:, :], kk[:, :], av[:, :], ALU.mult), f"ka{d}")
                    did(V.tensor_tensor(o[d][2][:, :], t1[:, :], e2[:, :], ALU.mult), f"kkap{d}")
                    did(V.tensor_tensor(o[d][3][:, :], kd[:, :], e2[:, :], ALU.mult), f"kp{d}")
                    did(V.scalar_tensor_tensor(out=t1[:, :], in0=kd[:, :], scalar=prm[:, 6:7], in1=r[:, :], op0=ALU.mult, op1=ALU.mult), f"bsrc{d}")
                pe_t.wait(dve, b, "bon1")
                dve.wait_ge(bonus_stored, (b + 1) * 16)
                act_t.wait(dve, b, "tok11")
                did(V.tensor_tensor(bon[:, :], flat[0], v[:, :], ALU.mult), "bonus")


def rwkv_scan(nc, R, S, vtok, chan_out):
    G = 8
    with Stage(nc) as st:
        X = [st.sb("kka_k", [64, 4, 2, P]) for _ in range(2)]
        Y = [st.sb("kk_r", [64, 4, 2, P]) for _ in range(2)]
        xt = [st.sb("kka_k_by_token", [P, 2, 4, 64]) for _ in range(2)]
        vt = [st.sb("v_by_token", [P, 4, 64]) for _ in range(2)]
        eg = [st.sb("edges", [64, 4, 2]) for _ in range(2)]
        state = [st.sb("state", [64, 4, 64]) for _ in range(G)]
        sref = st.sb("state_at_middle", [64, 4, 64])
        na, qb, ak, qk = (st.sb(n, [P, 4, P]) for n in ("minus_a", "r_kka", "kk_k", "r_k"))
        rhs, nsa = st.sb("rhs", [P, 4, 64]), st.sb("minus_sa", [P, 4, 64])
        y_sb = st.sb("y_out", [64, 4, P])
        inv = Inverse(nc, st, R["join_masks"])
        for d in range(2):
            for k in range(LEVELS):
                inv.joins[d, k] = st.sb("join", [P, 4, P])
        pa = st.ps("kka_products", [P, 4, 2, P])
        pk = st.ps("k_products", [P, 4, 2, P])
        bank = lambda p, i, n: p[:, 2 * i:2 * i + 2, :, :].rearrange("p a b n -> p (a b n)")[:, 0:n]
        rhs_ps = bank(pa, 0, 256).rearrange("p (h n) -> p h n", h=4)
        sa_ps = bank(pa, 1, 256).rearrange("p (h n) -> p h n", h=4)
        y_ps = bank(pk, 0, 512)[0:64].rearrange("p (h n) -> p h n", h=4)
        ds_ps = bank(pk, 1, 256)[0:64].rearrange("p (h n) -> p h n", h=4)
        loaded = [st.sem("group_loaded") for _ in range(2)]
        zeroed = st.sem("state_zeroed")
        y_stored = st.sem("y_stored")
        pe_t = Track(st.sem("tensor_did"), "pa pk rhs sa y ds", lead=2)
        act_t = Track(st.sem("scalar_did"), "rhs nsa y", lead=1)
        dve_t = Track(st.sem("vector_did"), "na qb ak qk sref sum state", lead=2)
        block = st.block()
        LOADS = 11 * 16

        @block.sync
        def _(sp):
            def load(it, g):
                d, q, s = g // 4, g % 4, g % 2
                t = tile_at(d, it)
                cols = slice(q * 256, q * 256 + 256)
                toks = bass.ds(t * P, P)
                dve_t.wait_last(sp, it * G + g - 1)
                for dst, i, name in ((X, 0, "kkap"), (X, 1, "kp"), (Y, 0, "kkp"), (Y, 1, "rp")):
                    sp.dma_start(dst[s][:, :, i, :], S[name][d][cols, toks].rearrange("(h p) t -> p h t", p=64)).then_inc(loaded[s], 16)
                for i, name in enumerate(("kkatok", "ktok2")):
                    sp.dma_start(xt[s][:, i, :, :].rearrange("p h n -> p (h n)"), S[name][d][toks, cols]).then_inc(loaded[s], 16)
                sp.dma_start(vt[s][:, :, :].rearrange("p h n -> p (h n)"), vtok[toks, cols]).then_inc(loaded[s], 16)
                with nc.allow_non_contiguous_dma("2 values a partition"):
                    for h in range(4):
                        sp.dma_start(eg[s][:, h, :], S["edges"][d][q * 256 + h * 64:q * 256 + h * 64 + 64, :, bass.ds(t, 1)
                                                                   ].rearrange("p e o -> p (e o)")).then_inc(loaded[s], 16)

            def store(it, g):
                d, q = g // 4, g % 4
                t = tile_at(d, it)
                act_t.wait(sp, it * G + g, "y")
                sp.dma_start(chan_out[d][q * 256:q * 256 + 256, bass.ds(t * P, P)].rearrange("(h p) t -> p h t", p=64),
                             y_sb[:, :, :]).then_inc(y_stored, 16)

            sp.sem_inc(y_stored, 16)
            with sp.Fori(0, NT) as it:
                load(it, 0)
                for g in range(1, G):
                    load(it, g)
                    store(it, g - 1)
                store(it, G - 1)
            sp.wait_ge(y_stored, (NT * G + 1) * 16)

        @block.gpsimd
        def _(pool):
            for g in range(G):
                nc.gpsimd.memset(state[g][:, :, :], 0.0).then_inc(zeroed, 1)

        @block.tensor
        def _(pe):
            pe_t.start(pe)
            pe.wait_ge(inv.joins_set, 2 * LEVELS)
            pe.wait_ge(zeroed, G)
            with pe.Fori(0, NT) as it:
                for g in range(G):
                    u, s, d = it * G + g, g % 2, g // 4
                    inv.dir = d
                    pe.wait_ge(loaded[s], (it * (G // 2) + g // 2 + 1) * LOADS)
                    for p, i, name in ((pa, 0, "pa"), (pk, 1, "pk")):
                        if i == 1:
                            dve_t.wait_last(pe, u)
                            act_t.wait_last(pe, u)
                        for h in range(4):
                            last = nc.tensor.matmul(p[:, h, :, :].rearrange("p a n -> p (a n)"), X[s][:, h, i, :],
                                                    Y[s][:, h, :, :].rearrange("p a n -> p (a n)"), start=True, stop=True)
                        pe_t.done(last, name)

                    def right_side():
                        dve_t.wait(pe, u, "sref")
                        for h in range(4):
                            nc.tensor.matmul(rhs_ps[:, h, :], Y[s][:, h, 0, :], sref[:, h, :], start=True, stop=False)
                            last = nc.tensor.matmul(rhs_ps[:, h, :], ak[:, h, :], vt[s][:, h, :], start=False, stop=True)
                        pe_t.done(last, "rhs")

                    dve_t.wait(pe, u, "na")
                    inv.tensor(pe, u, na, R["ident"], {4: right_side})
                    act_t.wait(pe, u, "rhs")
                    inv.wait_kept(pe, u)
                    for h in range(4):
                        last = nc.tensor.matmul(sa_ps[:, h, :], inv.transposed(h), rhs[:, h, :], start=True, stop=True)
                    pe_t.done(last, "sa")
                    act_t.wait(pe, u, "nsa")
                    for h in range(4):
                        out = y_ps[:, h, :]
                        nc.tensor.matmul(out, vt[s][:, h, :], qk[:, h, :], start=True, stop=False)
                        nc.tensor.matmul(out, sref[:, h, :], Y[s][:, h, 1, :], start=False, stop=False)
                        last = nc.tensor.matmul(out, nsa[:, h, :], qb[:, h, :], start=False, stop=True)
                    pe_t.done(last, "y")
                    for h in range(4):
                        out = ds_ps[:, h, :]
                        nc.tensor.matmul(out, xt[s][:, 1, h, :], vt[s][:, h, :], start=True, stop=False)
                        last = nc.tensor.matmul(out, xt[s][:, 0, h, :], nsa[:, h, :], start=False, stop=True)
                    pe_t.done(last, "ds")

        @block.scalar
        def _(act):
            act_t.start(act)
            with act.Fori(0, NT) as it:
                for g in range(G):
                    u = it * G + g
                    inv.dir = g // 4

                    def keep_right_side():
                        pe_t.wait(act, u, "rhs")
                        act_t.done(nc.scalar.copy(rhs[:, :, :], rhs_ps), "rhs")

                    inv.scalar(act, u, {4: keep_right_side})
                    pe_t.wait(act, u, "sa")
                    act_t.done(nc.scalar.activation(nsa[:, :, :], sa_ps, ACT.Identity, scale=-1.0), "nsa")
                    pe_t.wait(act, u, "y")
                    act.wait_ge(y_stored, (u + 1) * 16)
                    act_t.done(nc.scalar.copy(y_sb[:, :, :], y_ps), "y")

        @block.vector
        def _(dve):
            V = nc.vector
            dve_t.start(dve)
            for join in inv.joins.values():
                V.tensor_copy(join[:, :, :], R["ident"][:, :].rearrange("p (o n) -> p o n", o=1).to_broadcast([P, 4, P])
                              ).then_inc(inv.joins_set, 1)
            dve.wait_ge(inv.joins_set, 2 * LEVELS)
            dve.wait_ge(zeroed, G)
            with dve.Fori(0, NT) as it:
                for g in range(G):
                    u, s, d = it * G + g, g % 2, g // 4
                    inv.dir = d
                    strict = R["strict"][:, d:d + 1, :].to_broadcast([P, 4, P])
                    incl = R["incl"][:, d:d + 1, :].to_broadcast([P, 4, P])
                    pe_t.wait(dve, u, "pa")
                    dve_t.done(V.tensor_scalar(na[:, :, :], pa[:, :, 0, :], -1.0, None, ALU.mult), "na")

                    def rates_of_queries():
                        dve_t.done(V.tensor_tensor(qb[:, :, :], pa[:, :, 1, :], incl, ALU.mult), "qb")

                    def keys_before():
                        pe_t.wait(dve, u, "pk")
                        dve_t.done(V.tensor_tensor(ak[:, :, :], pk[:, :, 0, :], strict, ALU.mult), "ak")

                    def keys_of_queries():
                        dve_t.done(V.tensor_tensor(qk[:, :, :], pk[:, :, 1, :], incl, ALU.mult), "qk")

                    def state_at_middle():
                        dve.wait_ge(loaded[s], (it * (G // 2) + g // 2 + 1) * LOADS)
                        dve_t.done(V.tensor_tensor(sref[:, :, :], state[g][:, :, :], eg[s][:, :, 0:1].to_broadcast([64, 4, 64]), ALU.mult), "sref")

                    inv.vector(dve, u, {0: rates_of_queries, 1: keys_before, 2: keys_of_queries, 3: state_at_middle})
                    pe_t.wait(dve, u, "ds")
                    dve_t.wait(dve, u, "sref")
                    dve_t.done(V.tensor_tensor(state[g][:, :, :], sref[:, :, :], ds_ps, ALU.add), "sum")
                    dve_t.wait(dve, u, "sum")
                    dve_t.done(V.tensor_tensor(state[g][:, :, :], state[g][:, :, :], eg[s][:, :, 1:2].to_broadcast([64, 4, 64]), ALU.mult), "state")




def gla_prepare(nc, a, R, S, w):
    H, NCH, RANK = 4, T // GC, 16
    with Stage(nc) as st:
        wq, wk = st.sb("wq_slot", [P, KC, P]), st.sb("wk_slot", [P, KC, P])
        wg = st.sb("rank_weights", [P, KC, 2, RANK])
        gr = [st.sb("rank_rows", [RANK, T]) for _ in range(2)]
        w2 = st.sb("w_g2", [RANK, 2, P])
        bg = st.sb("b_g", [P, 2])
        keep = st.sb("keep", [P, T])
        q, k, v, m, e, c = (st.sb(n, [P, T]) for n in ("q", "k", "logits", "scratch", "exp_c", "c"))
        o = [[st.sb("result", [P, T]) for _ in range(2)] for _ in range(2)]
        tok = st.sb("by_token", [P, NT, P])
        ends = st.sb("edge_logs", [P, 2, NCH])
        edge = [st.sb("edges", [P, 2, NCH]) for _ in range(2)]
        ps = [st.ps("ps", [P, 3, 512]) for _ in range(2)]
        flat = [p[:, :, :].rearrange("p b n -> p (b n)")[:, 0:T] for p in ps]
        keep_s, wg_in, rank_s, rank_kept = st.sem("keep_set"), st.sem("rank_weights_in"), st.sem("rank_ready"), st.sem("rank_kept")
        loaded = st.sem("head_loaded")
        stored = [st.sem("direction_stored") for _ in range(2)]
        STORES = 4 * 16
        pe_t = Track(st.sem("tensor_did"), "q k g0 t0 g1 t1", lead=1)
        act_t = Track(st.sem("scalar_did"), "q1 q0 k1 k0 " + " ".join(f"e{d} l{d} edge{d} ec{d} em{d} tok{d}" for d in range(2)))
        dve_t = Track(st.sem("vector_did"), " ".join(f"v{d} abs{d} sp{d} g{d} scan{d} mid{d} end{d} cref{d} qp{d} kp{d}" for d in range(2)), lead=1)
        block = st.block()

        @block.sync
        def _(sp):
            sp.dma_start(wg[:, :, :, :].rearrange("p k n r -> p k (n r)"), w[:, 3072:3104].rearrange("(k p) c -> p k c", p=P)).then_inc(wg_in, 16)
            for d in range(2):
                sp.sem_inc(stored[d], STORES)
            with sp.Fori(0, H) as h:
                pe_t.wait_last(sp, h)
                sp.dma_start(wq[:, :, :], block_of(w[:, 0:512], h)).then_inc(loaded, 16)
                sp.dma_start(wk[:, :, :], block_of(w[:, 512:1024], h)).then_inc(loaded, 16)
                sp.dma_start(w2[:, :, :], a["gla_w_g2"][0].rearrange("n r c -> r n c")[:, :, bass.ds(h * P, P)]).then_inc(loaded, 16)
                with nc.allow_non_contiguous_dma("one value a partition"):
                    for d in range(2):
                        sp.dma_start(bg[:, d:d + 1], a["gla_b_g"][0, d][bass.ds(h * P, P)].rearrange("(p o) -> p o", o=1)).then_inc(loaded, 16)
                for d in range(2):
                    rows = bass.ds(h * P, P)
                    dve_t.wait(sp, h, f"kp{d}")
                    for i, name in enumerate(("qp", "kp")):
                        sp.dma_start(S[name][d][rows, :], o[d][i][:, :]).then_inc(stored[d], 16)
                    act_t.wait(sp, h, f"tok{d}")
                    sp.dma_start(S["gedges"][d][rows, :, :], edge[d][:, :, :]).then_inc(stored[d], 16)
                    sp.dma_start(S["ktok"][d].rearrange("(t p) c -> p t c", p=P)[:, :, rows], tok[:, :, :]).then_inc(stored[d], 16)
            for d in range(2):
                sp.wait_ge(stored[d], (H + 1) * STORES)

        @block.tensor
        def _(pe):
            pe_t.start(pe)
            pe.wait_ge(wg_in, 16)
            for d in range(2):
                for kc in range(KC):
                    for bank, (t0, n) in enumerate(NATURAL):
                        last = nc.tensor.matmul(ps[d][0:RANK, bank, 0:n], wg[:, kc, d, :], R["hT"][:, kc, t0:t0 + n],
                                                start=kc == 0, stop=kc == KC - 1)
                last.then_inc(rank_s, 1)
            pe.wait_ge(rank_kept, 2)
            with pe.Fori(0, H) as h:
                pe.wait_ge(loaded, (h + 1) * 5 * 16)
                dve_t.wait_last(pe, h)
                pe_t.done(product(nc, ps[0], wq, R["hT"]), "q")
                pe_t.done(product(nc, ps[1], wk, R["hT"]), "k")
                for d in range(2):
                    act_t.wait(pe, h, "q0" if d == 0 else "tok0")
                    if d == 1:
                        dve_t.wait(pe, h, "kp0")
                    for bank, (t0, n) in enumerate(NATURAL):
                        last = nc.tensor.matmul(ps[0][:, bank, 0:n], w2[:, d, :], gr[d][:, t0:t0 + n], start=True, stop=True)
                    pe_t.done(last, f"g{d}")
                    act_t.wait(pe, h, "k0")
                    dve_t.wait(pe, h, f"kp{d}")
                    for t in range(NT):
                        last = nc.tensor.transpose(flat[1][:, t * P:(t + 1) * P], o[d][1][:, t * P:(t + 1) * P], R["ident"][:, :])
                    pe_t.done(last, f"t{d}")

        @block.scalar
        def _(act):
            A = nc.scalar.activation
            for d in range(2):
                act.wait_ge(rank_s, d + 1)
                nc.scalar.copy(gr[d][:, :], flat[d][0:RANK, :]).then_inc(rank_kept, 1)
            with act.Fori(0, H) as h:
                dve_t.wait_last(act, h)
                pe_t.wait(act, h, "q")
                for part, t0, n in ((1, 0, TC), (0, TC, TX)):
                    act_t.done(A(q[:, t0:t0 + n], in_psum(ps[0], part), ACT.Identity, scale=P ** -0.5), f"q{part}")
                pe_t.wait(act, h, "k")
                for part, t0, n in ((1, 0, TC), (0, TC, TX)):
                    act_t.done(nc.scalar.copy(k[:, t0:t0 + n], in_psum(ps[1], part)), f"k{part}")
                for d in range(2):
                    dve_t.wait(act, h, f"abs{d}")
                    act_t.done(A(e[:, :], m[:, :], ACT.Exp, scale=-1.0), f"e{d}")
                    act_t.wait(act, h, f"e{d}")
                    act_t.done(A(e[:, :], e[:, :], ACT.Ln, bias=1.0), f"l{d}")
                    dve_t.wait(act, h, f"cref{d}")
                    act.wait_ge(stored[d], (h + 1) * STORES)
                    act_t.done(A(edge[d][:, :, :], ends[:, :, :], ACT.Exp), f"edge{d}")
                    act_t.done(A(e[:, :], c[:, :], ACT.Exp), f"ec{d}")
                    act_t.done(A(m[:, :], c[:, :], ACT.Exp, scale=-1.0), f"em{d}")
                    pe_t.wait(act, h, f"t{d}")
                    act.wait_ge(stored[1 - d], (h + 1 + d) * STORES)
                    act_t.done(nc.scalar.copy(tok[:, :, :].rearrange("p t n -> p (t n)"), flat[1]), f"tok{d}")

        @block.vector
        def _(dve):
            V = nc.vector
            dve_t.start(dve)
            V.memset(keep[:, :], 1.0).then_inc(keep_s, 1)
            dve.wait_ge(keep_s, 1)
            V.memset(keep[:, :].rearrange("p (t n) -> p t n", n=GC)[:, :, 0:1], 0.0).then_inc(keep_s, 1)
            dve.wait_ge(keep_s, 2)
            with dve.Fori(0, H) as h:
                def did(ins, name):
                    dve_t.done(ins, name)
                    dve_t.wait(dve, h, name)

                dve.wait_ge(loaded, (h + 1) * 5 * 16)
                for d in range(2):
                    f = direction(d)
                    by_chunk = lambda x: x[:, :].rearrange("p (t n) -> p t n", n=GC)
                    mid, end = (GC // 2, GC - 1) if d == 0 else (GC // 2 - 1, 0)
                    pe_t.wait(dve, h, f"g{d}")
                    did(V.tensor_scalar(v[:, :], flat[0], bg[:, d:d + 1], -1.0, ALU.add, ALU.mult), f"v{d}")
                    did(V.scalar_tensor_tensor(out=m[:, :], in0=v[:, :], scalar=-1.0, in1=v[:, :], op0=ALU.mult, op1=ALU.max), f"abs{d}")
                    act_t.wait(dve, h, f"l{d}")
                    did(V.scalar_tensor_tensor(out=v[:, :], in0=v[:, :], scalar=0.0, in1=e[:, :], op0=ALU.max, op1=ALU.add), f"sp{d}")
                    did(V.tensor_scalar(v[:, :], v[:, :], -1.0 / 16.0, None, ALU.mult), f"g{d}")
                    did(V.tensor_tensor_scan(out=c[:, f], data0=keep[:, :], data1=v[:, f], initial=0.0, op0=ALU.mult, op1=ALU.add), f"scan{d}")
                    did(V.tensor_copy(ends[:, 0, :], by_chunk(c)[:, :, mid]), f"mid{d}")
                    did(V.tensor_tensor(ends[:, 1, :], by_chunk(c)[:, :, end], ends[:, 0, :], ALU.subtract), f"end{d}")
                    did(V.tensor_tensor(by_chunk(c), by_chunk(c), ends[:, 0, :].rearrange("p (t o) -> p t o", o=1).to_broadcast([P, NCH, GC]),
                                        ALU.subtract), f"cref{d}")
                    dve.wait_ge(stored[d], (h + 1) * STORES)
                    act_t.wait(dve, h, f"ec{d}")
                    did(V.tensor_tensor(o[d][0][:, :], q[:, :], e[:, :], ALU.mult), f"qp{d}")
                    act_t.wait(dve, h, f"em{d}")
                    did(V.tensor_tensor(o[d][1][:, :], k[:, :], m[:, :], ALU.mult), f"kp{d}")


def gla_scan(nc, R, S, chan_out):
    H, DV, NCH, CTXC = 4, 256, T // GC, TC // GC
    G = 2
    with Stage(nc) as st:
        X = [st.sb("k_q_by_channel", [P, 2, H, GC]) for _ in range(2)]
        kt = [st.sb("k_by_token", [GC, H, P]) for _ in range(2)]
        vt = [st.sb("v_by_token", [GC, H, DV]) for _ in range(2)]
        eg = [st.sb("edges", [P, H, 2]) for _ in range(2)]
        state = [st.sb("state", [P, H, DV]) for _ in range(G)]
        sref = st.sb("state_at_middle", [P, H, DV])
        att = [st.sb("attention", [GC, H, GC]) for _ in range(G)]
        o_sb = [st.sb("o_out", [P, H, 2, GC]) for _ in range(2)]
        tick = st.sb("tick", [1, 1])
        att_ps = st.ps("attention_ps", [GC, H, GC])
        o_ps = st.ps("o_ps", [P, H, 2, GC])
        ds_ps = st.ps("update_ps", [P, H, DV])
        loaded = [st.sem("group_loaded") for _ in range(2)]
        zeroed = st.sem("zeroed")
        o_stored = [st.sem("o_stored") for _ in range(2)]
        pe_t = Track(st.sem("tensor_did"), "att o ds", lead=2)
        act_t = Track(st.sem("scalar_did"), "sref o", lead=1)
        dve_t = Track(st.sem("vector_did"), "att att2 sum state", lead=2)
        block = st.block()
        LOADS = 8 * 16

        def chunk_at(d, it):
            return it if d == 0 else (it * (NCH - 1) + CTXC - 1) % NCH

        @block.sync
        def _(sp):
            def load(it, g):
                c = chunk_at(g, it)
                toks = bass.ds(c * GC, GC)
                dve_t.wait_last(sp, it * G + g - 1)
                for i, name in ((0, "kp"), (1, "qp")):
                    sp.dma_start(X[g][:, i, :, :], S[name][g][:, toks].rearrange("(h p) t -> p h t", p=P)).then_inc(loaded[g], 16)
                sp.dma_start(kt[g][:, :, :].rearrange("p h n -> p (h n)"), S["ktok"][g][toks, :]).then_inc(loaded[g], 16)
                sp.dma_start(vt[g][:, :, :].rearrange("p h n -> p (h n)"), S["gvtok"][toks, :]).then_inc(loaded[g], 16)
                with nc.allow_non_contiguous_dma("2 values a partition"):
                    for h in range(H):
                        sp.dma_start(eg[g][:, h, :], S["gedges"][g][h * P:(h + 1) * P, :, bass.ds(c, 1)].rearrange("p e o -> p (e o)")
                                     ).then_inc(loaded[g], 16)

            def store(it, g):
                c = chunk_at(g, it)
                act_t.wait(sp, it * G + g, "o")
                sp.dma_start(chan_out[g][:, bass.ds(c * GC, GC)].rearrange("(h p) t -> p h t", p=P),
                             o_sb[g][:, :, :, :].rearrange("p h b n -> p (h b) n")).then_inc(o_stored[g], 16)

            for g in range(G):
                sp.sem_inc(o_stored[g], 16)
            with sp.Fori(0, NCH) as it:
                load(it, 0)
                load(it, 1)
                store(it, 0)
                store(it, 1)
            for g in range(G):
                sp.wait_ge(o_stored[g], (NCH + 1) * 16)

        def half(d):
            return (slice(0, GC // 2), slice(GC // 2, GC))[::1 if d == 0 else -1]

        @block.gpsimd
        def _(pool):
            for g in range(G):
                nc.gpsimd.memset(state[g][:, :, :], 0.0).then_inc(zeroed, 1)
                nc.gpsimd.memset(att[g][:, :, :], 0.0).then_inc(zeroed, 1)

        @block.tensor
        def _(pe):
            pe_t.start(pe)
            pe.wait_ge(zeroed, 2 * G)
            with pe.Fori(0, NCH) as it:
                for g in range(G):
                    u = it * G + g
                    pe.wait_ge(loaded[g], (it + 1) * LOADS)
                    dve_t.wait_last(pe, u)
                    act_t.wait_last(pe, u)
                    early, late = half(g)
                    for h in range(H):
                        nc.tensor.matmul(att_ps[:, h, late], X[g][:, 0, h, :], X[g][:, 1, h, late], start=True, stop=True)
                        last = nc.tensor.matmul(att_ps[early, h, early], X[g][:, 0, h, early], X[g][:, 1, h, early], start=True, stop=True)
                    pe_t.done(last, "att")
                    dve_t.wait(pe, u, "att2")
                    act_t.wait(pe, u, "sref")
                    for h in range(H):
                        for b in range(2):
                            nc.tensor.matmul(o_ps[:, h, b, :], sref[:, h, b * P:(b + 1) * P], X[g][:, 1, h, :], start=True, stop=False)
                            last = nc.tensor.matmul(o_ps[:, h, b, :], vt[g][:, h, b * P:(b + 1) * P], att[g][:, h, :], start=False, stop=True)
                    pe_t.done(last, "o")
                    for h in range(H):
                        last = nc.tensor.matmul(ds_ps[:, h, :], kt[g][:, h, :], vt[g][:, h, :], start=True, stop=True)
                    pe_t.done(last, "ds")

        @block.scalar
        def _(act):
            act_t.start(act)
            act.wait_ge(zeroed, 2 * G)
            with act.Fori(0, NCH) as it:
                for g in range(G):
                    u = it * G + g
                    act.wait_ge(loaded[g], (it + 1) * LOADS)
                    dve_t.wait_last(act, u)
                    for h in range(H):
                        last = nc.scalar.activation(sref[:, h, :], state[g][:, h, :], ACT.Identity, scale=eg[g][:, h, 0:1])
                    act_t.done(last, "sref")
                    pe_t.wait(act, u, "o")
                    act.wait_ge(o_stored[g], (it + 1) * 16)
                    act_t.done(nc.scalar.copy(o_sb[g][:, :, :, :], o_ps[:, :, :, :]), "o")

        @block.vector
        def _(dve):
            V = nc.vector
            dve_t.start(dve)
            dve.wait_ge(zeroed, 2 * G)
            with dve.Fori(0, NCH) as it:
                for g in range(G):
                    u = it * G + g
                    pe_t.wait(dve, u, "att")
                    V.memset(tick[:, :], 0.0)
                    early, late = half(g)
                    for rows, cols, name in ((slice(0, GC), late, "att"), (early, early, "att2")):
                        mask = R["mask64"][rows, g:g + 1, cols].to_broadcast([rows.stop - rows.start, H, GC // 2])
                        dve_t.done(V.copy_predicated(att[g][rows, :, cols], mask, att_ps[rows, :, cols]), name)
                    pe_t.wait(dve, u, "ds")
                    act_t.wait(dve, u, "sref")
                    dve_t.done(V.tensor_tensor(state[g][:, :, :], sref[:, :, :], ds_ps[:, :, :], ALU.add), "sum")
                    dve_t.wait(dve, u, "sum")
                    dve_t.done(V.tensor_tensor(state[g][:, :, :], state[g][:, :, :], eg[g][:, :, 1:2].to_broadcast([P, H, DV]), ALU.mult), "state")


def finish(nc, R, S, gain, gain_per_pair, rows, width, eps, pair=False, shift=None):
    names = "sum " + ("mean " if shift is not None else "") + "eps inv norm "
    names += "bonus " if shift is not None else ""
    per = [n + str(s) for s in range(2) for n in (names + "out").split()]
    order = sorted(per, key=lambda n: int(n[-1])) if not pair else ["sum0", "sum1", "eps0", "inv0", "norm0", "norm1", "out0", "out1"]
    with Stage(nc) as st:
        o, ob, z, sq = ([st.sb(n, [P, T]) for _ in range(2)] for n in ("o", "o_backward", "z", "squares"))
        bonus = [st.sb("bonus", [P, T]) for _ in range(2)] if shift is not None else None
        ga = st.sb("gain", [P, 2, 2])
        ps = [st.ps("sum_ps", [P, 3, 512]) for _ in range(2)]
        flat = [p[:, :, :].rearrange("p b n -> p (b n)")[:, 0:T] for p in ps]
        loaded = [st.sem("block_loaded") for _ in range(2)]
        dve_t = Track(st.sem("vector_did"), " ".join(order), lead=1)
        act_names = [n + str(s) for s in range(2) for n in ("sq", "root") + (("affine",) if shift is not None else ())]
        if pair:
            act_names = ["sq0", "sq1", "root0"]
        act_t = Track(st.sem("scalar_did"), " ".join(act_names))
        pe_names = [n + str(s) for s in range(2) for n in (("mean",) if shift is not None else ()) + ("sq",)]
        if pair:
            pe_names = ["sq0"]
        pe_t = Track(st.sem("tensor_did"), " ".join(pe_names))
        block = st.block()
        LOADS = 16 * (4 if shift is None else 6)

        @block.sync
        def _(sp):
            with sp.Fori(0, KC // 2) as it:
                for s in range(2):
                    c = bass.ds(it * (2 * P) + s * P, P)
                    dve_t.wait(sp, it - 1, f"out{s}")
                    sources = [(o, S["of"]), (ob, S["ob"]), (z, S["zT"])] + ([(bonus, S["bonusT"])] if shift is not None else [])
                    for dst, src in sources:
                        sp.dma_start(dst[s][:, :], src[c, :]).then_inc(loaded[s], 16)
                    with nc.allow_non_contiguous_dma("one value a partition"):
                        gc = c if gain_per_pair else slice(s * P % gain.shape[0], s * P % gain.shape[0] + P)
                        sp.dma_start(ga[:, s, 0:1], gain[gc].rearrange("(p o) -> p o", o=1)).then_inc(loaded[s], 16)
                        if shift is not None:
                            sp.dma_start(ga[:, s, 1:2], shift[gc].rearrange("(p o) -> p o", o=1)).then_inc(loaded[s], 16)

        @block.tensor
        def _(pe):
            def sums(out, moving, start=True, stop=True):
                for bank, (t0, n) in enumerate(NATURAL):
                    last = nc.tensor.matmul(out[:, bank, 0:n], rows[:, :], moving[:, t0:t0 + n], start=start, stop=stop)
                return last

            with pe.Fori(0, KC // 2) as it:
                if pair:
                    act_t.wait(pe, it, "sq1")
                    sums(ps[0], sq[0], stop=False)
                    pe_t.done(sums(ps[0], sq[1], start=False), "sq0")
                else:
                    for s in range(2):
                        if shift is not None:
                            dve_t.wait(pe, it, f"sum{s}")
                            pe_t.done(sums(ps[s], o[s]), f"mean{s}")
                        act_t.wait(pe, it, f"sq{s}")
                        pe_t.done(sums(ps[s], sq[s]), f"sq{s}")

        @block.scalar
        def _(act):
            A = nc.scalar.activation
            with act.Fori(0, KC // 2) as it:
                def square(s):
                    dve_t.wait(act, it, f"mean{s}" if shift is not None else f"sum{s}")
                    act_t.done(A(sq[s][:, :], o[s][:, :], ACT.Square), f"sq{s}")

                def root(s):
                    dve_t.wait(act, it, f"eps{s}")
                    act_t.done(A(ob[s][:, :], ob[s][:, :], ACT.Sqrt), f"root{s}")

                if pair:
                    square(0)
                    square(1)
                    root(0)
                else:
                    for s in range(2):
                        square(s)
                        root(s)
                        if shift is not None:
                            dve_t.wait(act, it, f"norm{s}")
                            act_t.done(A(o[s][:, :], o[s][:, :], ACT.Identity, bias=ga[:, s, 1:2], scale=ga[:, s, 0:1]), f"affine{s}")

        @block.vector
        def _(dve):
            V = nc.vector
            dve_t.start(dve)
            with dve.Fori(0, KC // 2) as it:
                def did(ins, name):
                    dve_t.done(ins, name)
                    dve_t.wait(dve, it, name)

                out = [R["hT"][:, bass.ds(it * 2 + s, 1), :].rearrange("p o t -> p (o t)") for s in range(2)]

                def step(name, s):
                    if name == "sum":
                        dve.wait_ge(loaded[s], (it + 1) * LOADS)
                        did(V.tensor_tensor(o[s][:, :], o[s][:, :], ob[s][:, :], ALU.add), f"sum{s}")
                    elif name == "mean":
                        pe_t.wait(dve, it, f"mean{s}")
                        did(V.scalar_tensor_tensor(out=o[s][:, :], in0=flat[s], scalar=-1.0 / width, in1=o[s][:, :],
                                                   op0=ALU.mult, op1=ALU.add), f"mean{s}")
                    elif name == "eps":
                        pe_t.wait(dve, it, f"sq{s}")
                        did(V.tensor_scalar(ob[s][:, :], flat[s], 1.0 / width, eps, ALU.mult, ALU.add), f"eps{s}")
                    elif name == "inv":
                        act_t.wait(dve, it, f"root{s}")
                        did(V.reciprocal(ob[s][:, :], ob[s][:, :]), f"inv{s}")
                    elif name == "norm":
                        did(V.tensor_tensor(o[s][:, :], o[s][:, :], ob[0 if pair else s][:, :], ALU.mult), f"norm{s}")
                    elif name == "bonus":
                        act_t.wait(dve, it, f"affine{s}")
                        did(V.tensor_tensor(o[s][:, :], o[s][:, :], bonus[s][:, :], ALU.add), f"bonus{s}")
                    elif shift is not None:
                        did(V.tensor_tensor(out[s], o[s][:, :], z[s][:, :], ALU.mult), f"out{s}")
                    else:
                        did(V.scalar_tensor_tensor(out=out[s], in0=o[s][:, :], scalar=ga[:, s, 0:1], in1=z[s][:, :],
                                                   op0=ALU.mult, op1=ALU.mult), f"out{s}")

                for name in order:
                    step(name[:-1], int(name[-1]))


RQ, RK = 3, 2
ROPE, NOPE = 64, 128
MLA_SCALE = (NOPE + ROPE) ** -0.5


def mla_project(nc, a, R, qn, kvn, kr):
    w = a["mla_w_in"][0]
    with Stage(nc) as st:
        w_sb = [st.sb("w_slot", [P, KC, P]) for _ in range(2)]
        wr = st.sb("w_rope", [P, KC, ROPE])
        norms = st.sb("norm_gains", [P, RQ + RK])
        cs = st.sb("cos_sin", [ROPE, 2, TX])
        turned = st.sb("turned_rope", [ROPE, TX])
        sq = [st.sb("squares", [P, T]) for _ in range(2)]
        rs = [st.sb("inverse_root", [P, T]) for _ in range(2)]
        ps = [st.ps("product_ps", [P, 3, 512]) for _ in range(2)]
        flat = [p[:, :, :].rearrange("p b n -> p (b n)")[:, 0:T] for p in ps]
        w_in = [st.sem("w_loaded") for _ in range(2)]
        small_in = st.sem("small_loaded")
        mm, kept, squared, sums = st.sem("product_ready"), st.sem("kept"), st.sem("squared"), st.sem("square_sums_ready")
        eps_s, root, step_s = st.sem("eps_added"), st.sem("root_ready"), st.sem("vector_step")
        block = st.block()
        blocks = [qn[:, i, :] for i in range(RQ)] + [kvn[:, i, :] for i in range(RK)]
        N = RQ + RK

        @block.sync
        def _(sp):
            sp.dma_start(wr[:, :, :], w[:, N * P:N * P + ROPE].rearrange("(k p) c -> p k c", p=P)).then_inc(small_in, 16)
            sp.dma_start(cs[:, :, :], a["c_cos_sin"]).then_inc(small_in, 16)
            with nc.allow_non_contiguous_dma("5 values a partition"):
                sp.dma_start(norms[:, 0:RQ], a["mla_q_norm"][0].rearrange("(k p) -> p k", p=P)).then_inc(small_in, 16)
                sp.dma_start(norms[:, RQ:N], a["mla_kv_norm"][0].rearrange("(k p) -> p k", p=P)).then_inc(small_in, 16)
            for c in range(N):
                if c >= 2:
                    sp.wait_ge(mm, c - 1)
                sp.dma_start(w_sb[c % 2][:, :, :], w[:, c * P:(c + 1) * P].rearrange("(k p) c -> p k c", p=P)).then_inc(w_in[c % 2], 16)

        def natural(out, weights, moving):
            for bank, (t0, n) in enumerate(NATURAL):
                for kc in range(KC):
                    last = nc.tensor.matmul(out[:, bank, 0:n], weights[:, kc, :], moving[:, kc, t0:t0 + n],
                                            start=kc == 0, stop=kc == KC - 1)
            return last

        @block.tensor
        def _(pe):
            for c in range(N):
                pe.wait_ge(w_in[c % 2], 16 * (c // 2 + 1))
                if c >= 2:
                    pe.wait_ge(kept, c - 1)
                natural(ps[c % 2], w_sb[c % 2], R["hT"]).then_inc(mm, 1)
            pe.wait_ge(small_in, 64)
            pe.wait_ge(kept, N - 1)
            natural(ps[1][0:ROPE], wr, R["hT"]).then_inc(mm, 1)
            pe.wait_ge(kept, N + 1)
            for i in range(2):
                last = nc.tensor.matmul(ps[0][0:ROPE, i, :], R["swap"][:, :], kr[:, TC + i * 512:TC + (i + 1) * 512], start=True, stop=True)
            last.then_inc(mm, 1)
            for c in range(N):
                pe.wait_ge(squared, c + 1)
                first, end = c in (0, RQ), c in (RQ - 1, N - 1)
                if c == 0:
                    pe.wait_ge(step_s, 2)
                out = ps[0] if c < RQ else ps[1]
                for bank, (t0, n) in enumerate(NATURAL):
                    last = nc.tensor.matmul(out[:, bank, 0:n], R["ones"][:, :], sq[c % 2][:, t0:t0 + n], start=first, stop=end)
                last.then_inc(sums, 1)

        @block.scalar
        def _(act):
            for c in range(N):
                act.wait_ge(mm, c + 1)
                nc.scalar.copy(blocks[c], flat[c % 2]).then_inc(kept, 1)
            act.wait_ge(mm, N + 1)
            nc.scalar.copy(kr[:, :], flat[1][0:ROPE, :]).then_inc(kept, 1)
            for c in range(N):
                if c >= 2:
                    act.wait_ge(sums, c - 1)
                act.wait_ge(kept, c + 1)
                nc.scalar.activation(sq[c % 2][:, :], blocks[c], ACT.Square).then_inc(squared, 1)
            for i in range(2):
                act.wait_ge(eps_s, i + 1)
                nc.scalar.activation(rs[i][:, :], rs[i][:, :], ACT.Sqrt).then_inc(root, 1)

        @block.vector
        def _(dve):
            V = nc.vector
            step = Steps(dve, step_s)
            dve.wait_ge(small_in, 64)
            dve.wait_ge(mm, N + 2)
            step(V.tensor_tensor(turned[:, :], ps[0][0:ROPE, 0:2, :].rearrange("p b n -> p (b n)"), cs[:, 1, :], ALU.mult))
            step(V.tensor_tensor(kr[:, TC:T], kr[:, TC:T], cs[:, 0, :], ALU.mult))
            step(V.tensor_tensor(kr[:, TC:T], kr[:, TC:T], turned[:, :], ALU.add))
            for i, upto in ((0, RQ), (1, N)):
                dve.wait_ge(sums, upto)
                V.tensor_scalar(rs[i][:, :], flat[i], 1.0 / (P * (RQ, RK)[i]), 1e-6, ALU.mult, ALU.add).then_inc(eps_s, 1)
            for i in range(2):
                dve.wait_ge(root, i + 1)
                step(V.reciprocal(rs[i][:, :], rs[i][:, :]))
            dve.wait_ge(squared, N)
            for c in range(N):
                V.scalar_tensor_tensor(out=blocks[c], in0=blocks[c], scalar=norms[:, c:c + 1], in1=rs[0 if c < RQ else 1][:, :],
                                       op0=ALU.mult, op1=ALU.mult).then_inc(step_s, 1)


def mla_attention(nc, a, R, S, qn, kvn, kr):
    H, QT = 8, TX // P
    with Stage(nc) as st:
        wq = st.sb("w_queries", [P, RQ, NOPE + ROPE])
        wkv = st.sb("w_keys_values", [P, RK, 2 * P])
        cs = st.sb("cos_sin", [ROPE, 2, TX])
        q, qr, qt = st.sb("q", [P, TX]), st.sb("q_rope", [ROPE, TX]), st.sb("q_turned", [ROPE, TX])
        k, v, z = st.sb("k", [P, T]), st.sb("v", [P, NT, P]), st.sb("z", [P, TX])
        prob = st.sb("probabilities", [P, T])
        pt = st.sb("probabilities_turned", [P, NT, P])
        o = st.sb("o", [P, P])
        mx, nmx, total = (st.sb(n, [P, 1]) for n in ("row_max", "minus_max", "row_sum"))
        inv = [st.sb("inverse_sum", [P, 1]) for _ in range(2)]
        s_ps, t_ps = st.ps("scores_ps", [P, 3, 512]), st.ps("turned_ps", [P, 3, 512])
        o_ps, ot_ps = st.ps("o_ps", [P, P]), st.ps("o_turned_ps", [P, P])
        sf, tf = (x[:, :, :].rearrange("p b n -> p (b n)")[:, 0:T] for x in (s_ps, t_ps))
        cs_in, loaded, zeroed = st.sem("cos_sin_loaded"), st.sem("head_loaded"), st.sem("context_zeroed")
        late = lambda name, i: f" {name}{i - 1}" if i > 0 else ""
        pe_t = Track(st.sem("tensor_did"), "q qr k swap v s0" + "".join(
            f" t{i}" + (f" s{i + 1}" if i < QT - 1 else "") + late("ot", i) + f" o{i}" for i in range(QT)) + f" ot{QT - 1}")
        act_t = Track(st.sem("scalar_did"), "q qr k v" + "".join(f" exp{i}" + late("o", i) + f" pt{i}" for i in range(QT)) + f" o{QT - 1}", lead=1)
        dve_t = Track(st.sem("vector_did"), "cos sin rope" + "".join(f" max{i} nmx{i} inv{i}" + late("out", i) for i in range(QT))
                      + f" out{QT - 1}", lead=1)
        block = st.block()
        wuq, wukv = a["mla_w_uq"][0], a["mla_w_ukv"][0]

        @block.sync
        def _(sp):
            sp.dma_start(cs[:, :, :], a["c_cos_sin"]).then_inc(cs_in, 16)
            with sp.Fori(0, H) as h:
                dve_t.wait_last(sp, h)
                sp.dma_start(wq[:, :, :], block_of(wuq, h, NOPE + ROPE)).then_inc(loaded, 16)
                sp.dma_start(wkv[:, :, :], block_of(wukv, h, 2 * P)).then_inc(loaded, 16)
                sp.dma_start(z[:, :], S["zT"][bass.ds(h * P, P), TC:T]).then_inc(loaded, 16)

        @block.tensor
        def _(pe):
            with pe.Fori(0, H) as h:
                pe.wait_ge(loaded, (h + 1) * 48)
                dve_t.wait_last(pe, h)
                for cols, out, name in ((slice(0, NOPE), s_ps, "q"), (slice(NOPE, NOPE + ROPE), t_ps[0:ROPE], "qr")):
                    if name == "qr":
                        act_t.wait(pe, h, "q")
                    for i in range(TX // 512):
                        for c in range(RQ):
                            last = nc.tensor.matmul(out[:, i, :], wq[:, c, cols], qn[:, c, TC + i * 512:TC + (i + 1) * 512],
                                                    start=c == 0, stop=c == RQ - 1)
                    pe_t.done(last, name)
                act_t.wait(pe, h, "qr")
                for bank, (t0, n) in enumerate(NATURAL):
                    for c in range(RK):
                        last = nc.tensor.matmul(t_ps[:, bank, 0:n], wkv[:, c, 0:P], kvn[:, c, t0:t0 + n], start=c == 0, stop=c == RK - 1)
                pe_t.done(last, "k")
                for i in range(TX // 512):
                    last = nc.tensor.matmul(s_ps[0:ROPE, i, :], R["swap"][:, :], qr[:, i * 512:(i + 1) * 512], start=True, stop=True)
                pe_t.done(last, "swap")
                dve_t.wait(pe, h, "sin")
                for t in range(NT):
                    for c in range(RK):
                        last = nc.tensor.matmul(sf[:, t * P:(t + 1) * P], kvn[:, c, t * P:(t + 1) * P], wkv[:, c, P:2 * P],
                                                start=c == 0, stop=c == RK - 1)
                pe_t.done(last, "v")

                def scores(i):
                    for bank, (t0, n) in enumerate(NATURAL):
                        nc.tensor.matmul(s_ps[:, bank, 0:n], q[:, i * P:(i + 1) * P], k[:, t0:t0 + n], start=True, stop=False)
                        last = nc.tensor.matmul(s_ps[:, bank, 0:n], qr[:, i * P:(i + 1) * P], kr[:, t0:t0 + n], start=False, stop=True)
                    pe_t.done(last, f"s{i}")

                dve_t.wait(pe, h, "rope")
                act_t.wait(pe, h, "v")
                scores(0)

                def turn_output(i):
                    act_t.wait(pe, h, f"o{i}")
                    if i > 0:
                        dve_t.wait(pe, h, f"out{i - 1}")
                    pe_t.done(nc.tensor.transpose(ot_ps[:, :], o[:, :], R["ident"][:, :]), f"ot{i}")

                for i in range(QT):
                    act_t.wait(pe, h, f"exp{i}")
                    for t in range(NT):
                        last = nc.tensor.transpose(tf[:, t * P:(t + 1) * P], prob[:, t * P:(t + 1) * P], R["ident"][:, :])
                    pe_t.done(last, f"t{i}")
                    if i < QT - 1:
                        scores(i + 1)
                    if i > 0:
                        turn_output(i - 1)
                    act_t.wait(pe, h, f"pt{i}")
                    for t in range(NT):
                        last = nc.tensor.matmul(o_ps[:, :], pt[:, t, :], v[:, t, :], start=t == 0, stop=t == NT - 1)
                    pe_t.done(last, f"o{i}")
                turn_output(QT - 1)

        @block.scalar
        def _(act):
            A = nc.scalar.activation
            act_t.start(act)
            with act.Fori(0, H) as h:
                pe_t.wait(act, h, "q")
                act_t.done(nc.scalar.copy(q[:, :], sf[:, 0:TX]), "q")
                pe_t.wait(act, h, "qr")
                act_t.done(nc.scalar.copy(qr[:, :], tf[0:ROPE, 0:TX]), "qr")
                pe_t.wait(act, h, "k")
                act_t.done(nc.scalar.copy(k[:, :], tf), "k")
                pe_t.wait(act, h, "v")
                act_t.done(nc.scalar.copy(v[:, :, :].rearrange("p t n -> p (t n)"), sf), "v")

                def keep_output(i):
                    pe_t.wait(act, h, f"o{i}")
                    dve_t.wait(act, h, f"inv{i}")
                    act_t.done(A(o[:, :], o_ps[:, :], ACT.Identity, scale=inv[i % 2][:, :]), f"o{i}")

                for i in range(QT):
                    dve_t.wait(act, h, f"nmx{i}")
                    if i > 0:
                        dve_t.wait(act, h, f"inv{i - 1}")
                    act_t.done(A(prob[:, :], sf, ACT.Exp, bias=nmx[:, :], scale=MLA_SCALE, accum_out=total[:, :]), f"exp{i}")
                    if i > 0:
                        keep_output(i - 1)
                    pe_t.wait(act, h, f"t{i}")
                    act_t.done(nc.scalar.copy(pt[:, :, :].rearrange("p t n -> p (t n)"), tf), f"pt{i}")
                keep_output(QT - 1)

        @block.vector
        def _(dve):
            V = nc.vector
            V.memset(R["hT"][:, :, 0:TC], 0.0).then_inc(zeroed, 1)
            dve_t.start(dve)
            dve.wait_ge(cs_in, 16)
            with dve.Fori(0, H) as h:
                def did(ins, name):
                    dve_t.done(ins, name)
                    dve_t.wait(dve, h, name)

                dve.wait_ge(loaded, (h + 1) * 48)
                pe_t.wait(dve, h, "swap")
                did(V.tensor_tensor(qr[:, :], qr[:, :], cs[:, 0, :], ALU.mult), "cos")
                did(V.tensor_tensor(qt[:, :], sf[0:ROPE, 0:TX], cs[:, 1, :], ALU.mult), "sin")
                did(V.tensor_tensor(qr[:, :], qr[:, :], qt[:, :], ALU.add), "rope")

                def gate(i):
                    pe_t.wait(dve, h, f"ot{i}")
                    out = R["hT"][:, bass.ds(h, 1), TC + i * P:TC + (i + 1) * P].rearrange("p o t -> p (o t)")
                    did(V.tensor_tensor(out, ot_ps[:, :], z[:, i * P:(i + 1) * P], ALU.mult), f"out{i}")

                for i in range(QT):
                    pe_t.wait(dve, h, f"s{i}")
                    did(V.tensor_reduce(mx[:, :], sf, AX.X, ALU.max), f"max{i}")
                    did(V.tensor_scalar(nmx[:, :], mx[:, :], -MLA_SCALE, None, ALU.mult), f"nmx{i}")
                    act_t.wait(dve, h, f"exp{i}")
                    did(V.reciprocal(inv[i % 2][:, :], total[:, :]), f"inv{i}")
                    if i > 0:
                        gate(i - 1)
                gate(QT - 1)


def network(nc, a, out):
    with ExitStack() as es:
        R = {}
        shapes = dict(ident=[P, P], ones=[P, P], xT=[P, KC, T], hT=[P, KC, T], mod=[P, 2, 3 * KC], ln=[P, 2, KC],
                      strict=[P, 2, P], incl=[P, 2, P], head_ones=[P, P], off=[P, 2, P], swap=[ROPE, ROPE])
        for name, shape in shapes.items():
            R[name] = es.enter_context(nc.sbuf_tensor(name, shape, F32))
        R["join_masks"] = es.enter_context(nc.sbuf_tensor("join_masks", [P, 2 * LEVELS, P], U8))
        R["mod_ctx"] = es.enter_context(nc.sbuf_tensor("mod_ctx", [P, 2, KC], F32))
        R["chains_ctx"] = es.enter_context(nc.sbuf_tensor("chains_ctx", [P, TC // P, 2 * 2 * H], F32))
        R["mask64"] = es.enter_context(nc.sbuf_tensor("mask64", [GC, 2, GC], U8))

        def dram(name, *shape):
            return nc.dram_tensor("d_" + name, shape, F32, kind="Internal").ap()

        S = {n: dram(n, D, T) for n in ("zT", "of", "ob")}
        S["mods"] = dram("mods", 2, DEPTH, 3 * D)
        S["silu_ctx"], S["gate_w"] = dram("silu_ctx", D), dram("gate_w", D, 2 * H)
        outs = [S["of"], S["ob"]]
        load_constants(nc, a, R)
        modulation(nc, a, R, S)
        turn_in(nc, a, R)
        context_silu(nc, a, S)
        context_modulation(nc, a, R, S)

        modulate(nc, a, R, S, 0)
        G = {"qT": dram("gdn_qT", D, T), "kT": dram("gdn_kT", D, T), "ktok": dram("gdn_ktok", T, D),
             "vtok": dram("gdn_vtok", T, D), "gates": dram("gates", T, 2 * KINDS * H)}
        w, taps = a["gdn_w_in"][0], a["gdn_conv"][0]
        with ExitStack() as exact:
            logits = ContextLogits(nc, exact, a, R, S)
            gdn_channels(nc, a, R, w[:, 0:D], taps[:, 0:D], KC, logits, norm=P ** -0.5, chan_out=G["qT"])
            gdn_channels(nc, a, R, w[:, D:2 * D], taps[:, D:2 * D], KC, logits, norm=1.0, chan_out=G["kT"], tok_out=G["ktok"])
            gdn_channels(nc, a, R, w[:, 2 * D:3 * D], taps[:, 2 * D:3 * D], KC, logits, tok_out=G["vtok"])
            silu_channels(nc, a, R, w[:, 3 * D:4 * D], KC, S["zT"], logits)
            assert logits.piece == PIECES
        gdn_gates(nc, a, R, w[:, 4 * D:4 * D + 32], a["gdn_a_log"][0], a["gdn_dt_bias"][0], G["gates"])
        gdn_scan(nc, R, G, outs)
        finish(nc, R, S, a["gdn_norm"][0], False, R["ones"], P, 1e-6)
        put_out(nc, a, R, a["gdn_w_out"][0], 0, True)

        modulate(nc, a, R, S, 1)
        for n in ("rT", "kT", "vT", "bonusT"):
            S[n] = dram("rwkv_" + n, D, T)
        W = {"vtok": dram("rwkv_vtok", T, D)}
        for n in ("kkp", "rp", "kkap", "kp"):
            W[n] = [dram(f"rwkv_{n}{d}", D, T) for d in range(2)]
        for n in ("kkatok", "ktok2"):
            W[n] = [dram(f"rwkv_{n}{d}", T, D) for d in range(2)]
        W["edges"] = [dram(f"rwkv_edges{d}", D, 2, NT) for d in range(2)]
        with ExitStack() as low:
            lw, la = (low.enter_context(nc.sbuf_tensor(n, [P, T], F32)) for n in ("rwkv_decay_rank", "rwkv_rate_rank"))
            with ExitStack() as mixing:
                xx, mx = (mixing.enter_context(nc.sbuf_tensor(n, [P, KC, T], F32)) for n in ("neighbours", "mixed"))
                M = {**R, "hT": mx}
                mu, w = a["rwkv_mu"][0], a["rwkv_w_rkvz"][0]
                shift_tokens(nc, R, xx)
                mix_tokens(nc, R, xx, mu[0], mx)
                plain_channels(nc, M, w[0], KC, chan_out=S["rT"])
                mix_tokens(nc, R, xx, mu[1], mx)
                low_rank(nc, M, [(0, a["rwkv_w1"][0, 0]), (64, a["rwkv_w1"][0, 1])], lw, True)
                mix_tokens(nc, R, xx, mu[2], mx)
                plain_channels(nc, M, w[1], KC, chan_out=S["kT"])
                mix_tokens(nc, R, xx, mu[3], mx)
                plain_channels(nc, M, w[2], KC, chan_out=S["vT"], tok_out=W["vtok"])
                mix_tokens(nc, R, xx, mu[4], mx)
                low_rank(nc, M, [(0, a["rwkv_a1"][0, 0]), (64, a["rwkv_a1"][0, 1])], la, False)
                mix_tokens(nc, R, xx, mu[5], mx)
                silu_channels(nc, a, M, w[3], KC, S["zT"])
            rwkv_prepare(nc, a, R, W, lw, la, S["rT"], S["kT"], S["vT"], S["bonusT"])
        rwkv_scan(nc, R, W, W["vtok"], outs)
        finish(nc, R, S, a["rwkv_gn_g"][0], True, R["head_ones"], 64, 64e-5, shift=a["rwkv_gn_b"][0])
        put_out(nc, a, R, a["rwkv_w_out"][0], 1, True)

        modulate(nc, a, R, S, 2)
        L = {"gvtok": dram("gla_vtok", T, D)}
        for n in ("qp", "kp"):
            L[n] = [dram(f"gla_{n}{d}", D // 2, T) for d in range(2)]
        L["ktok"] = [dram(f"gla_ktok{d}", T, D // 2) for d in range(2)]
        L["gedges"] = [dram(f"gla_edges{d}", D // 2, 2, T // GC) for d in range(2)]
        w = a["gla_w_in"][0]
        gla_prepare(nc, a, R, L, w)
        plain_channels(nc, R, w[:, D:2 * D], KC, tok_out=L["gvtok"])
        silu_channels(nc, a, R, w[:, 2 * D:3 * D], KC, S["zT"])
        gla_scan(nc, R, L, outs)
        finish(nc, R, S, a["gla_norm"][0], False, R["ones"], 2 * P, 1e-6, pair=True)
        put_out(nc, a, R, a["gla_w_out"][0], 2, True)

        modulate(nc, a, R, S, 3)
        with ExitStack() as low:
            qn, kvn, kr = (low.enter_context(nc.sbuf_tensor(n, s, F32)) for n, s in (
                ("q_low_rank", [P, RQ, T]), ("kv_low_rank", [P, RK, T]), ("k_rope", [ROPE, T])))
            mla_project(nc, a, R, qn, kvn, kr)
            silu_channels(nc, a, R, a["mla_w_in"][0][:, 704:704 + D], KC, S["zT"])
            mla_attention(nc, a, R, S, qn, kvn, kr)
        put_out(nc, a, R, a["mla_w_out"][0], 3, False)
        turn_out(nc, R, out)


def constants():
    i = np.arange(P)
    before, after = i[:, None] <= i[None, :], i[:, None] >= i[None, :]
    both = lambda x, y: np.stack([x, y], 1)
    j = np.arange(GC)
    joins = [(i[:, None] // 2 ** k - i[None, :] // 2 ** k == (1, -1)[d]) & (i[:, None] // 2 ** (k + 1) == i[None, :] // 2 ** (k + 1))
             for d in range(2) for k in range(LEVELS)]
    half = ROPE // 2
    swap = np.zeros((ROPE, ROPE), np.float32)
    swap[np.arange(half) + half, np.arange(half)] = -1.0
    swap[np.arange(half), np.arange(half) + half] = 1.0
    freq = (np.float32(10000.0) ** (-np.arange(half // 2, dtype=np.float32) / np.float32(half // 2))).astype(np.float32)
    token = np.arange(TX)
    angle = np.concatenate([(token // 64).astype(np.float32)[:, None] * freq, (token % 64).astype(np.float32)[:, None] * freq], 1)
    angle = np.concatenate([angle, angle], 1).T
    f = np.float32
    return {"ident": np.eye(P, dtype=f), "ones": np.ones((P, P), f),  "strict": both(i[:, None] < i[None, :], i[:, None] > i[None, :]).astype(f), "incl": both(before, after).astype(f),
            "head_ones": (i[:, None] // 64 == i[None, :] // 64).astype(f), "swap": swap,
            "off": both(np.where(before, 0, -1e30), np.where(after, 0, -1e30)).astype(f),
            "join_masks": np.stack(joins, 1).astype(f),
            "mask64": both(j[:, None] <= j[None, :], j[:, None] >= j[None, :]).astype(f),
            "cos_sin": both(np.cos(angle), np.sin(angle)).astype(f)}


def kernel(**inputs):
    import concourse.bacc as bacc
    from concourse.bass_utils import run_bass_kernel_spmd

    nc = bacc.Bacc("TRN2", target_bir_lowering=False, num_devices=1)
    arrays = {name: np.ascontiguousarray(x) for name, x in inputs.items()}
    arrays.update({"c_" + name: x for name, x in constants().items()})
    a = {name: nc.dram_tensor(name, x.shape, mybir.dt.from_np(x.dtype), kind="ExternalInput").ap() for name, x in arrays.items()}
    out = nc.dram_tensor("out", (1, TX, D), F32, kind="ExternalOutput").ap()
    network(nc, a, out)
    results = run_bass_kernel_spmd(nc, [arrays], core_ids=[0])
    return results.results[0]["out"]
```
